# Optimizing a Trainium2 kernel written in Bass

```python
import math
import jax
import jax.numpy as jnp
from jax import lax
import numpy as np

D_MODEL = 1024
BATCH = 1
SEQ = 128
DEPTH = 2
DEC_BATCH = 1
DEC_SEQ = 512
PAST_LEN = 128

GRID_W = 64
ROPE_THETA = 10000.0
NORM_EPS = 1e-6
Q_BLOCK = 128
NEG_INF = -1e30

DIFF_HEADS = 4
DIFF_QK_DIM = 64
DIFF_V_DIM = 2 * DIFF_QK_DIM
MLA_HEADS = 8
MLA_Q_RANK = 384
MLA_KV_RANK = 256
MLA_NOPE_DIM = 64
MLA_ROPE_DIM = 32
MLA_V_DIM = 64
AB_IN_SIZES = (DIFF_HEADS * 2 * DIFF_QK_DIM, DIFF_HEADS * 2 * DIFF_QK_DIM, DIFF_HEADS * DIFF_V_DIM,
               MLA_Q_RANK, MLA_KV_RANK, MLA_ROPE_DIM)
AB_IN = sum(AB_IN_SIZES)
AB_OUT = DIFF_HEADS * DIFF_V_DIM + MLA_HEADS * MLA_V_DIM
SWA_HEADS = 16
SWA_KV_HEADS = 4
SWA_GROUP = SWA_HEADS // SWA_KV_HEADS
SWA_HEAD_DIM = 64
WINDOW = 128
SWA_OUT = SWA_HEADS * SWA_HEAD_DIM
SWA_IN = SWA_OUT + 2 * SWA_KV_HEADS * SWA_HEAD_DIM
N_EXPERTS = 16
N_GROUPS = 4
EXPERTS_PER_GROUP = N_EXPERTS // N_GROUPS
TOP_K = 2
D_EXPERT = 256

N_AB_LAYERS = (DEPTH + 1) // 2
N_SWA_LAYERS = DEPTH // 2

kernel_name = "hybrid_diffusion_prefix_trunk_step"

F32 = jnp.float32

def _split(x, sizes):
    bounds, acc = [], 0
    for s in sizes[:-1]:
        acc += s
        bounds.append(acc)
    return jnp.split(x, bounds, axis=-1)

def rmsnorm(x, g):
    xf = x.astype(F32)
    y = xf * lax.rsqrt(jnp.mean(xf * xf, axis=-1, keepdims=True) + NORM_EPS)
    return (y * g.astype(F32)).astype(x.dtype)

def ada_mod(cond, w, b):
    m = jax.nn.silu(cond) @ w + b
    return jnp.split(m[:, None, :], 6, axis=-1)

def modulate(x, g, shift, scale):
    return rmsnorm(x, g) * (1.0 + scale) + shift

def axial_rope(n_tokens, rot_dim):
    n_rows = n_tokens // GRID_W
    rows = jnp.repeat(jnp.arange(n_rows), GRID_W)
    cols = jnp.tile(jnp.arange(GRID_W), n_rows)
    n_freq = rot_dim // 4
    inv = ROPE_THETA ** (-jnp.arange(n_freq, dtype=F32) / n_freq)
    ang = jnp.concatenate([rows[:, None] * inv, cols[:, None] * inv], axis=-1)
    return jnp.cos(ang), jnp.sin(ang)

def apply_rope(x, cos, sin):
    extra = x.ndim - 3
    cos = cos.reshape(cos.shape[0], *([1] * extra), cos.shape[1]).astype(x.dtype)
    sin = sin.reshape(sin.shape[0], *([1] * extra), sin.shape[1]).astype(x.dtype)
    x1, x2 = x[..., 0::2], x[..., 1::2]
    return jnp.stack([x1 * cos - x2 * sin, x1 * sin + x2 * cos], axis=-1).reshape(x.shape)

def block_attention(q, k, v, sink=None):
    b, sq, hk, r, d = q.shape
    nb = sq // Q_BLOCK
    qb = jnp.moveaxis(q.reshape(b, nb, Q_BLOCK, hk, r, d), 1, 0)
    kf, vf = k.astype(F32), v.astype(F32)
    scale = d ** -0.5

    def one(qi):
        s = jnp.einsum('bqhrd,bkhd->bhrqk', qi.astype(F32), kf) * scale
        if sink is not None:
            sk = jnp.broadcast_to(sink.astype(F32)[None, :, :, None, None], s.shape[:-1] + (1,))
            p = jax.nn.softmax(jnp.concatenate([s, sk], axis=-1), axis=-1)[..., :-1]
        else:
            p = jax.nn.softmax(s, axis=-1)
        return jnp.einsum('bhrqk,bkhe->bqhre', p, vf)

    o = lax.map(one, qb)
    return jnp.moveaxis(o, 0, 1).reshape(b, sq, hk, r, v.shape[-1]).astype(q.dtype)

def window_attention(q, k, v, k_ctx, v_ctx, sink):
    b, n, hk, r, d = q.shape
    nb = n // Q_BLOCK
    band = Q_BLOCK + 2 * WINDOW
    pad = ((0, 0), (WINDOW, WINDOW), (0, 0), (0, 0))
    kp, vp = jnp.pad(k.astype(F32), pad), jnp.pad(v.astype(F32), pad)
    kc, vc = k_ctx.astype(F32), v_ctx.astype(F32)
    qb = jnp.moveaxis(q.reshape(b, nb, Q_BLOCK, hk, r, d), 1, 0)
    scale = d ** -0.5
    sink_f = sink.astype(F32)[None, :, :, None, None]

    def one(args):
        i, qi = args
        start = i * Q_BLOCK
        kb = lax.dynamic_slice_in_dim(kp, start, band, axis=1)
        vb = lax.dynamic_slice_in_dim(vp, start, band, axis=1)
        qpos = start + jnp.arange(Q_BLOCK)
        kpos = start - WINDOW + jnp.arange(band)
        valid = ((jnp.abs(qpos[:, None] - kpos[None, :]) <= WINDOW)
                 & (kpos >= 0)[None, :] & (kpos < n)[None, :])
        qf = qi.astype(F32)
        s_loc = jnp.where(valid, jnp.einsum('bqhrd,bkhd->bhrqk', qf, kb) * scale, NEG_INF)
        s_ctx = jnp.einsum('bqhrd,bkhd->bhrqk', qf, kc) * scale
        s_sink = jnp.broadcast_to(sink_f, s_ctx.shape[:-1] + (1,))
        p = jax.nn.softmax(jnp.concatenate([s_loc, s_ctx, s_sink], axis=-1), axis=-1)
        return (jnp.einsum('bhrqk,bkhe->bqhre', p[..., :band], vb)
                + jnp.einsum('bhrqk,bkhe->bqhre', p[..., band:-1], vc))

    o = lax.map(one, (jnp.arange(nb), qb))
    return jnp.moveaxis(o, 0, 1).reshape(b, n, hk, r, v.shape[-1]).astype(q.dtype)

def diff_lambda_value(lam_p, lambda_init):
    lp = lam_p.astype(F32)
    return jnp.exp(jnp.sum(lp[0] * lp[1])) - jnp.exp(jnp.sum(lp[2] * lp[3])) + lambda_init

def ab_project(h, w_in, q_norm_g, w_qb, kv_norm_g):
    b, s, _ = h.shape
    qa, ka, va, q_lat, ckv, k_rope = _split(h @ w_in, AB_IN_SIZES)
    qa = qa.reshape(b, s, DIFF_HEADS, 2, DIFF_QK_DIM)
    ka = ka.reshape(b, s, DIFF_HEADS, 2, DIFF_QK_DIM)
    va = va.reshape(b, s, DIFF_HEADS, DIFF_V_DIM)
    qb = (rmsnorm(q_lat, q_norm_g) @ w_qb).reshape(b, s, MLA_HEADS, MLA_NOPE_DIM + MLA_ROPE_DIM)
    return qa, ka, va, qb, rmsnorm(ckv, kv_norm_g), k_rope

def ab_mix(qa, ka, va, qb, ckv, k_rope, lam, lambda_init, subln_g, w_kvb, w_out):
    b, s = qa.shape[:2]
    n_keys = ka.shape[1]
    qd = qa.reshape(b, s, 2 * DIFF_HEADS, 1, DIFF_QK_DIM)
    kd = ka.reshape(b, n_keys, 2 * DIFF_HEADS, DIFF_QK_DIM)
    vd = jnp.repeat(va, 2, axis=2)
    od = block_attention(qd, kd, vd).reshape(b, s, DIFF_HEADS, 2, DIFF_V_DIM)
    od = od[:, :, :, 0] - lam.astype(od.dtype) * od[:, :, :, 1]
    od = rmsnorm(od, subln_g) * (1.0 - lambda_init)
    kv = (ckv @ w_kvb).reshape(b, n_keys, MLA_HEADS, MLA_NOPE_DIM + MLA_V_DIM)
    k_nope, vb = kv[..., :MLA_NOPE_DIM], kv[..., MLA_NOPE_DIM:]
    kb = jnp.concatenate(
        [k_nope, jnp.broadcast_to(k_rope[:, :, None, :], (b, n_keys, MLA_HEADS, MLA_ROPE_DIM))], axis=-1)
    ob = block_attention(qb[:, :, :, None, :], kb, vb)
    mixed = jnp.concatenate([od.reshape(b, s, -1), ob.reshape(b, s, -1)], axis=-1)
    return mixed @ w_out

def swa_project(h, w_in):
    b, s, _ = h.shape
    q, k, v = _split(h @ w_in, (SWA_OUT, SWA_KV_HEADS * SWA_HEAD_DIM, SWA_KV_HEADS * SWA_HEAD_DIM))
    return (q.reshape(b, s, SWA_KV_HEADS, SWA_GROUP, SWA_HEAD_DIM),
            k.reshape(b, s, SWA_KV_HEADS, SWA_HEAD_DIM),
            v.reshape(b, s, SWA_KV_HEADS, SWA_HEAD_DIM))

def moe_ffn(h, router_w, router_bias, w_gate, w_up, w_down):
    scores = jax.nn.sigmoid(h.astype(F32) @ router_w.astype(F32))
    sel = (scores + router_bias.astype(F32)).reshape(*scores.shape[:-1], N_GROUPS, EXPERTS_PER_GROUP)
    group_score = lax.top_k(sel, TOP_K)[0].sum(axis=-1)
    gidx = lax.top_k(group_score, 1)[1][..., 0]
    in_group = jnp.einsum('bsge,bsg->bse', sel, jax.nn.one_hot(gidx, N_GROUPS, dtype=F32))
    local = lax.top_k(in_group, TOP_K)[1]
    eidx = gidx[..., None] * EXPERTS_PER_GROUP + local
    w = jnp.take_along_axis(scores, eidx, axis=-1)
    w = w / jnp.sum(w, axis=-1, keepdims=True)
    gates = jnp.einsum('bske,bsk->bse', jax.nn.one_hot(eidx, N_EXPERTS, dtype=F32), w).astype(h.dtype)
    g = jnp.einsum('bsd,edf->bsef', h, w_gate)
    u = jnp.einsum('bsd,edf->bsef', h, w_up)
    a = jax.nn.silu(g) * u * gates[..., None]
    return jnp.einsum('bsef,efd->bsd', a, w_down)

def setup_inputs(seed: int = 0) -> dict:
    key = jax.random.key(seed)
    kit = iter(jax.random.split(key, 40))
    d = D_MODEL

    def nrm(shape, s=1.0):
        return jax.random.normal(next(kit), shape, F32) * s

    def gain(shape):
        return 1.0 + nrm(shape, 0.02)

    return {
        "x_prompt": nrm((BATCH, SEQ, d)),
        "x_sample": nrm((DEC_BATCH, DEC_SEQ, d)),
        "cache_diff_k": nrm((DEC_BATCH, N_AB_LAYERS, PAST_LEN, DIFF_HEADS, 2, DIFF_QK_DIM)),
        "cache_diff_v": nrm((DEC_BATCH, N_AB_LAYERS, PAST_LEN, DIFF_HEADS, DIFF_V_DIM)),
        "cache_mla_ckv": nrm((DEC_BATCH, N_AB_LAYERS, PAST_LEN, MLA_KV_RANK)),
        "cache_mla_krope": nrm((DEC_BATCH, N_AB_LAYERS, PAST_LEN, MLA_ROPE_DIM)),
        "cache_swa_k": nrm((DEC_BATCH, N_SWA_LAYERS, PAST_LEN, SWA_KV_HEADS, SWA_HEAD_DIM)),
        "cache_swa_v": nrm((DEC_BATCH, N_SWA_LAYERS, PAST_LEN, SWA_KV_HEADS, SWA_HEAD_DIM)),
        "c": nrm((DEC_BATCH, d)),
        "c_ctx": nrm((d,)),
        "ada_w": nrm((DEPTH, d, 6 * d), 0.5 * d ** -0.5),
        "ada_b": nrm((DEPTH, 6 * d), 0.02),
        "norm1_g": gain((DEPTH, d)),
        "norm2_g": gain((DEPTH, d)),
        "final_norm_g": gain((d,)),
        "ab_w_in": nrm((N_AB_LAYERS, d, AB_IN), d ** -0.5),
        "diff_lambda": nrm((N_AB_LAYERS, 4, DIFF_QK_DIM), 0.1),
        "diff_subln_g": gain((N_AB_LAYERS, DIFF_V_DIM)),
        "mla_q_norm_g": gain((N_AB_LAYERS, MLA_Q_RANK)),
        "mla_w_qb": nrm((N_AB_LAYERS, MLA_Q_RANK, MLA_HEADS * (MLA_NOPE_DIM + MLA_ROPE_DIM)), MLA_Q_RANK ** -0.5),
        "mla_kv_norm_g": gain((N_AB_LAYERS, MLA_KV_RANK)),
        "mla_w_kvb": nrm((N_AB_LAYERS, MLA_KV_RANK, MLA_HEADS * (MLA_NOPE_DIM + MLA_V_DIM)), MLA_KV_RANK ** -0.5),
        "ab_w_out": nrm((N_AB_LAYERS, AB_OUT, d), AB_OUT ** -0.5),
        "swa_w_in": nrm((N_SWA_LAYERS, d, SWA_IN), d ** -0.5),
        "swa_sink": nrm((N_SWA_LAYERS, SWA_HEADS), 0.5),
        "swa_w_out": nrm((N_SWA_LAYERS, SWA_OUT, d), SWA_OUT ** -0.5),
        "router_w": nrm((d, N_EXPERTS), d ** -0.5),
        "router_bias": nrm((N_EXPERTS,), 0.01),
        "moe_w_gate": nrm((DEPTH, N_EXPERTS, d, D_EXPERT), d ** -0.5),
        "moe_w_up": nrm((DEPTH, N_EXPERTS, d, D_EXPERT), d ** -0.5),
        "moe_w_down": nrm((DEPTH, N_EXPERTS, D_EXPERT, d), D_EXPERT ** -0.5),
    }

def reference(x_prompt, x_sample, cache_diff_k, cache_diff_v, cache_mla_ckv, cache_mla_krope,
              cache_swa_k, cache_swa_v, c, c_ctx, ada_w, ada_b, norm1_g, norm2_g, final_norm_g,
              ab_w_in, diff_lambda, diff_subln_g, mla_q_norm_g, mla_w_qb, mla_kv_norm_g, mla_w_kvb,
              ab_w_out, swa_w_in, swa_sink, swa_w_out, router_w, router_bias,
              moe_w_gate, moe_w_up, moe_w_down):
    n_lat = x_sample.shape[1]
    cos_d, sin_d = axial_rope(n_lat, DIFF_QK_DIM)
    cos_r, sin_r = axial_rope(n_lat, MLA_ROPE_DIM)
    cos_s, sin_s = axial_rope(n_lat, SWA_HEAD_DIM)
    cond_ctx = c_ctx[None, :]
    xp, xs = x_prompt, x_sample
    diff_k_l, diff_v_l, ckv_l, krope_l, swa_k_l, swa_v_l = [], [], [], [], [], []

    for l in range(DEPTH):
        sh1_p, sc1_p, g1_p, sh2_p, sc2_p, g2_p = ada_mod(cond_ctx, ada_w[l], ada_b[l])
        sh1_s, sc1_s, g1_s, sh2_s, sc2_s, g2_s = ada_mod(c, ada_w[l], ada_b[l])
        hp = modulate(xp, norm1_g[l], sh1_p, sc1_p)
        hs = modulate(xs, norm1_g[l], sh1_s, sc1_s)
        j = l // 2
        if l % 2 == 0:
            lambda_init = 0.8 - 0.6 * math.exp(-0.3 * l)
            lam = diff_lambda_value(diff_lambda[j], lambda_init)
            qa, ka, va, qb, ckv, kr = ab_project(hp, ab_w_in[j], mla_q_norm_g[j], mla_w_qb[j], mla_kv_norm_g[j])
            diff_k_l.append(ka)
            diff_v_l.append(va)
            ckv_l.append(ckv)
            krope_l.append(kr)
            mp = ab_mix(qa, ka, va, qb, ckv, kr, lam, lambda_init, diff_subln_g[j], mla_w_kvb[j], ab_w_out[j])
            qa, ka, va, qb, ckv, kr = ab_project(hs, ab_w_in[j], mla_q_norm_g[j], mla_w_qb[j], mla_kv_norm_g[j])
            qa = apply_rope(qa, cos_d, sin_d)
            ka = apply_rope(ka, cos_d, sin_d)
            qb = jnp.concatenate([qb[..., :MLA_NOPE_DIM], apply_rope(qb[..., MLA_NOPE_DIM:], cos_r, sin_r)], axis=-1)
            kr = apply_rope(kr, cos_r, sin_r)
            ms = ab_mix(qa,
                        jnp.concatenate([ka, cache_diff_k[:, j]], axis=1),
                        jnp.concatenate([va, cache_diff_v[:, j]], axis=1),
                        qb,
                        jnp.concatenate([ckv, cache_mla_ckv[:, j]], axis=1),
                        jnp.concatenate([kr, cache_mla_krope[:, j]], axis=1),
                        lam, lambda_init, diff_subln_g[j], mla_w_kvb[j], ab_w_out[j])
        else:
            sink = swa_sink[j].reshape(SWA_KV_HEADS, SWA_GROUP)
            qp, kp, vp = swa_project(hp, swa_w_in[j])
            swa_k_l.append(kp)
            swa_v_l.append(vp)
            op = block_attention(qp, kp, vp, sink)
            mp = op.reshape(op.shape[0], op.shape[1], SWA_OUT) @ swa_w_out[j]
            qs, ks, vs = swa_project(hs, swa_w_in[j])
            qs = apply_rope(qs, cos_s, sin_s)
            ks = apply_rope(ks, cos_s, sin_s)
            o_s = window_attention(qs, ks, vs, cache_swa_k[:, j], cache_swa_v[:, j], sink)
            ms = o_s.reshape(o_s.shape[0], o_s.shape[1], SWA_OUT) @ swa_w_out[j]
        xp = xp + g1_p * mp
        xs = xs + g1_s * ms
        hp = modulate(xp, norm2_g[l], sh2_p, sc2_p)
        hs = modulate(xs, norm2_g[l], sh2_s, sc2_s)
        xp = xp + g2_p * moe_ffn(hp, router_w, router_bias, moe_w_gate[l], moe_w_up[l], moe_w_down[l])
        xs = xs + g2_s * moe_ffn(hs, router_w, router_bias, moe_w_gate[l], moe_w_up[l], moe_w_down[l])

    y_prompt = rmsnorm(xp, final_norm_g)
    y_sample = rmsnorm(xs, final_norm_g)
    new_diff_k = jnp.stack(diff_k_l, axis=1)
    new_diff_v = jnp.stack(diff_v_l, axis=1)
    new_mla_ckv = jnp.stack(ckv_l, axis=1)
    new_mla_krope = jnp.stack(krope_l, axis=1)
    new_swa_k = jnp.stack(swa_k_l, axis=1)
    new_swa_v = jnp.stack(swa_v_l, axis=1)
    return (y_prompt, y_sample, new_diff_k, new_diff_v, new_mla_ckv, new_mla_krope, new_swa_k, new_swa_v)


_drawn_inputs = setup_inputs


def setup_inputs(seed=0):
    import zlib

    import numpy as np

    out = dict(_drawn_inputs(seed))
    spreads = {}
    factors = {'cache_mla_ckv': 3.252,
     'cache_mla_krope': 4.511,
     'final_norm_g': 21.649,
     'diff_lambda': 3.155,
     'diff_subln_g': 33.523,
     'mla_q_norm_g': 8.0,
     'mla_kv_norm_g': 2.864,
     'swa_sink': 8.0,
     'cache_swa_k': 3.086,
     'cache_swa_v': 2.978,
     'norm2_g': 3.311,
     'router_bias': 2.946}
    for name, (base, spread) in spreads.items():
        noise = np.random.default_rng([zlib.crc32(name.encode()), seed]).standard_normal(out[name].shape)
        drawn = base * np.exp(spread * noise) if base else spread * noise
        out[name] = jnp.asarray(drawn.astype(out[name].dtype))
    for name, factor in factors.items():
        out[name] = (out[name] * factor).astype(out[name].dtype)
    return out
```

```python
import math
from contextlib import ExitStack

import numpy as np

import concourse.bass as bass
from concourse import mybir

F32 = mybir.dt.float32
I32 = mybir.dt.int32
ALU = mybir.AluOpType
ACT = mybir.ActivationFunctionType
AX_X = mybir.AxisListType.X

P = 128
D = 1024
KC = D // P
MT = 5
PROMPT = 4
KT = 6
CACHE_KT, PROMPT_KT = 4, 5
NKEY = KT * P
AB_IN = 2208
QL, CKV, KR = 384, 256, 32
MH, NOPE, MQ = 8, 64, 96
E, F = 16, 256
NG, EPG = 4, 4
NT = (MT * P * 2 + E * (P - 1)) // P
EPS = 1e-6
NEG = -1e30
LAMBDA_INIT = 0.8 - 0.6 * math.exp(-0.3 * 0)
SWA_IN = 1536
KB = 256

(C_ID, C_TRI, C_ONE, C_M1, C_M2, C_C64, C_S64, C_C32, C_S32, C_THR, C_IOTA, C_LE, C_CODE, C_TOK, C_SCL,
 NCONST) = np.cumsum([0, P, P, P, P, P, 256, 256, P, P, 80, NT * E, E * E, 4, MT, 1]).tolist()


def constants():
    c = np.zeros((P, NCONST), np.float32)
    i = np.arange(P)
    c[:, C_ID:C_ID + P] = np.eye(P)
    c[:, C_TRI:C_TRI + P] = i[:, None] < i[None, :]
    c[:, C_ONE:C_ONE + P] = 1.0
    c[:, C_M1:C_M1 + P] = np.where(i[None, :] >= i[:, None], 0.0, NEG)
    c[:, C_M2:C_M2 + P] = np.where(i[None, :] <= i[:, None], 0.0, NEG)
    pos = np.arange(4 * P)
    for dim, cc, cs in ((64, C_C64, C_S64), (32, C_C32, C_S32)):
        nf = dim // 4
        inv = np.float32(10000.0) ** (-np.arange(nf, dtype=np.float32) / np.float32(nf))
        ang = np.concatenate([(pos // 64).astype(np.float32)[:, None] * inv,
                              (pos % 64).astype(np.float32)[:, None] * inv], -1)
        co = np.repeat(np.cos(ang), 2, -1)
        si = np.repeat(np.sin(ang), 2, -1)
        si[:, 0::2] *= -1
        for m in range(4):
            c[:, cc + m * dim:cc + (m + 1) * dim] = co[m * P:(m + 1) * P]
            c[:, cs + m * dim:cs + (m + 1) * dim] = si[m * P:(m + 1) * P]
    c[:, C_THR:C_THR + 80] = np.tile(np.arange(MT) * P, E)
    c[:, C_IOTA:C_IOTA + NT * E] = np.repeat(np.arange(NT), E)
    c[:, C_LE:C_LE + E * E] = (np.arange(E)[None, :] <= np.arange(E)[:, None]).reshape(-1)
    c[:, C_CODE:C_CODE + 4] = 4 - np.arange(4)
    c[:, C_TOK:C_TOK + MT] = i[:, None] + P * np.arange(MT)[None, :]
    c[:96, C_SCL] = np.isin(np.arange(96) % 48 // 8, (1, 4))
    return c


def attention_units(l):
    heads = [("diff", h) for h in range(8)] + [("mla", h) for h in range(8)] if l == 0 else \
        [("swa", h) for h in range(16)]
    units = []
    for p in range(len(heads) // 2):
        for m in range(MT):
            for kind, h in heads[2 * p:2 * p + 2]:
                if m == PROMPT:
                    kts = [PROMPT_KT]
                elif kind == "swa":
                    kts = [t for t in (m - 1, m, m + 1) if 0 <= t < 4] + [CACHE_KT]
                else:
                    kts = [0, 1, 2, 3, CACHE_KT]
                units.append((kind, m, h, kts))
    return units


def pieces(kts):
    out = []
    for j, t in enumerate(kts):
        if out and t == out[-1][1] + out[-1][2] and j % 4:
            out[-1][2] += 1
        else:
            out.append([j * P, t, 1])
    return out


def build(nc, x_prompt, x_sample, cache_diff_k, cache_diff_v, cache_mla_ckv, cache_mla_krope, cache_swa_k,
          cache_swa_v, c_s, c_ctx, ada_w, ada_b, norm1_g, norm2_g, final_norm_g, ab_w_in, diff_lambda,
          diff_subln_g, mla_q_norm_g, mla_w_qb, mla_kv_norm_g, mla_w_kvb, ab_w_out, swa_w_in, swa_sink,
          swa_w_out, router_w, router_bias, moe_w_gate, moe_w_up, moe_w_down, consts,
          y_prompt, y_sample, new_diff_k, new_diff_v, new_mla_ckv, new_mla_krope, new_swa_k, new_swa_v):
    with ExitStack() as ctx:
        def sb(name, shape, dt=F32):
            return ctx.enter_context(nc.sbuf_tensor(name, shape, dt))

        def sem(name):
            return ctx.enter_context(nc.semaphore(name))

        def per_layer(name):
            return [sem(f"{name}_l{l}") for l in range(2)]

        def scratch(name, shape, dt=F32):
            return nc.dram_tensor(name, shape, dt, kind="Internal").ap()

        class Repeated:

            def __init__(self, name, total):
                self.sem, self.total = sem(name), total

            def at(self, l, n):
                return l * self.total + n

        ps = ctx.enter_context(nc.psum_tensor("ps", [P, 8, 512], F32))

        X = sb("x_rows", [P, MT * D])
        H = sb("region_h", [P, 20 * KB])
        A = sb("region_a", [P, 80 * KB])
        B = sb("region_b", [P, 48 * KB])
        ST = sb("region_st", [P, 12 * KB])
        G = sb("region_g", [P, 8 * KB])
        cst = sb("cst", [P, NCONST])

        def view(region, at, *dims):
            v = region[:, at:at + int(np.prod(dims))]
            names = "abcd"[:len(dims)]
            if len(dims) > 1:
                v = v.rearrange(f"p ({' '.join(names)}) -> p {' '.join(names)}", **dict(zip(names[1:], dims[1:])))
            return v

        ident = cst[:, C_ID:C_ID + P]
        tri = cst[:, C_TRI:C_TRI + P]
        ones = cst[:, C_ONE:C_ONE + P]
        masks = {-1: cst[:, C_M1:C_M1 + P], 1: cst[:, C_M2:C_M2 + P]}

        x_rows = view(X, 0, MT, D)
        vd = view(X, 0, KT, 512)
        hT = view(H, 0, KC, MT * P)
        w_in = view(A, 0, KC, AB_IN)
        qaT = view(A, KC * AB_IN, 4, MT * P)
        qbT = view(A, 0, MH, MT * P)
        kbT = view(A, 20 * KB, MH, NKEY)
        vb = view(A, 44 * KB, KT, 512)
        w_swa = view(A, 0, KC, SWA_IN)
        w_swao = view(A, 48 * KB, KC, D)
        ada_ring = [[view(R, i * 16 * KB, KC, 512) for i in range(3)] for R in (B, A)]
        wqb = view(B, 0, 3, 768)
        wkvb = view(B, 9 * KB, 2, 1024)
        qlT = view(B, 17 * KB, 3, MT * P)
        krT = view(B, 17 * KB + 1920, NKEY)
        ckvT = view(B, 17 * KB + 1920 + 768, 2, NKEY)
        kaT = view(B, 34 * KB, 4, NKEY)
        w_abo = view(B, 0, KC, D)
        qsT = view(B, 0, 8, MT * P)
        ksT = view(B, 20 * KB, 4, NKEY)
        vs = view(B, 32 * KB, KT, 256)
        wg = [view(B, s * 24 * KB, KC, F) for s in range(2)]
        wu = [view(B, s * 24 * KB + 8 * KB, KC, F) for s in range(2)]
        wd = [view(B, s * 24 * KB + 16 * KB, 2, D) for s in range(2)]
        yc = [view(B, i * 4 * KB, D) for i in range(2 * MT)]
        radd = [view(ST, i * P, P) for i in range(2)]
        rmul = [view(ST, (2 + i) * P, P) for i in range(2)]
        arow = [view(ST, (4 + i) * P, P) for i in range(2)]
        acol = [view(ST, (6 + i) * P, 96) for i in range(2)]
        ada_out = [[view(A, KC * AB_IN + i * 512, 512) for i in range(2)], [view(ST, 8 * KB + i * 512, 512) for i in range(2)]]
        junk = view(ST, 4 * KB, D)
        qrow = view(ST, 0, 512)
        krow = view(ST, 2 * KB, 512)
        rtmp = view(ST, 4 * KB, 512)
        rtmp2 = view(ST, 6 * KB, 512)
        qlrow = view(ST, 8 * KB, QL)
        cvrow = view(ST, 8 * KB + QL, CKV + KR)
        qbrow = [view(ST, 0, 768), view(ST, 8 * KB, 768)]
        qsrow = view(ST, 0, D)
        ksrow = view(ST, 8 * KB, 4, 2, 64)
        prow = [view(ST, i * 644, 644) for i in range(2)]
        pT = [view(ST, 1288 + i * 640, MT, P) for i in range(2)]
        xn = [view(G, i * D, D) for i in range(2)]
        gate = xn
        bc = [view(A, at * KB, 4, D) for at in (56, 0)]
        xg = [[view(A, at * KB + i * D, D) for i in range(2)] for at in (72, 16)]
        xgT = [[view(A, at * KB + i * D, KC, P) for i in range(2)] for at in (48, 24)]
        yr = [view(H, i * D, D) for i in range(2)]
        aT = [view(H, 8 * KB + i * 2 * P, 2 * P) for i in range(2)]
        ebuf = [view(H, 10 * KB + i * 2 * P, 2 * P) for i in range(2)]
        rt = [12 * KB]

        def route_tmp(*dims):
            at = rt[0]
            rt[0] += int(np.prod(dims))
            assert rt[0] <= 20 * KB
            return view(H, at, *dims)

        sel, prod, o1, o2, mask = (route_tmp(MT, NG, EPG) for _ in range(5))
        pairs = route_tmp(MT * NG, 6)
        gs, goh, ing, ing2, oh1, oh2, eqt = (route_tmp(MT, 4) for _ in range(7))
        mx5 = route_tmp(MT)
        tot, cum, pref, slot = (route_tmp(MT, E) for _ in range(4))
        cnt, ntile, ends, starts = (route_tmp(E) for _ in range(4))
        thr_hit = route_tmp(E, MT)
        le_hit = route_tmp(E, E)
        cache_k = sb("cache_k_rows", [P, 512])
        cache_c = view(ST, 8 * KB + QL + CKV + KR, CKV + KR)
        sqj = sb("square_out", [P, 384])
        ckv_g = sb("ckv_g", [P, CKV])
        ada_cols = [sb(f"ada_cols{l}", [P, 96]) for l in range(2)]
        cin = sb("cond_in", [P, 2, KC])
        cex = sb("cond_exp", [P, 2, KC])
        csil = sb("cond_silu", [P, 2, KC])
        gcols = sb("gain_cols", [P, 4])
        rw = sb("router_w_sb", [P, KC, E])
        rbias = sb("router_bias_sb", [P, E])
        sink8 = sb("sink8", [P, 16])
        lam = sb("lam", [P, 8])
        ss = sb("sum_squares", [P, 16])
        var = sb("variance", [P, 16])
        rstd = sb("rstd", [P, 16])
        mhalf = sb("minus_half", [P, 16])
        nmx = sb("neg_max", [P, 4])
        mxs = sb("row_max", [P, 4])
        rsum = sb("row_sum", [P, 4])
        rrec = sb("row_rec", [P, 4])
        orow = sb("head_rows", [P, 2, P])
        o0 = sb("first_half", [P, P])
        osq = sb("head_squares", [P, P])
        scores = sb("scores", [P, MT, E])
        wsel = sb("wsel", [P, 4, MT])
        slots = sb("slots", [P, 2, MT], I32)
        eidf = sb("eid_f", [P, NT])
        eidi = sb("eid_i", [P, NT], I32)
        idrow = sb("slot_rows", [P, P])
        idall = sb("slot_ids", [P, NT], I32)
        idt = [sb(f"slot_ids_now{i}", [P, 1], I32) for i in range(2)]

        ada_rows = scratch("ada_rows", [2, 2, 6 * D])
        h2_dram = scratch("h2_rows", [MT * P, D])
        slot_dram = scratch("slot_tokens", [NT * P, 1])
        y_dram = scratch("expert_rows", [NT * P, D])

        ld_cst, ld_c, ld_x, ld_x2, ld_small, ld_mod = (sem(n) for n in ("ld_cst", "ld_c", "ld_x", "ld_x2", "ld_small", "ld_mod"))
        ld_ada = [sem(f"ld_ada{i}") for i in range(3)]
        ld_win, ld_lat, ld_cache, ld_vcache = (sem(n) for n in ("ld_win", "ld_lat", "ld_cache", "ld_vcache"))
        units = [attention_units(l) for l in range(2)]
        UNITS = len(units[0])
        assert UNITS == len(units[1])

        def wide(l, n):
            return sum(len(u[3]) == 5 for u in units[l][:n])

        ld_wout = Repeated("ld_wout", 16)
        ld_gate = Repeated("ld_gate", 32)
        ld_gate2 = Repeated("ld_gate2", 32)
        ld_bc = Repeated("ld_bc", 64)
        s_ss = Repeated("s_ss", MT)
        s_var = Repeated("s_var", 1)
        s_rstd = Repeated("s_rstd", 1)
        s_xn = Repeated("s_xn", MT)
        s_n1t = Repeated("s_n1t", MT)
        s_n1a = Repeated("s_n1a", MT)
        s_n1d = Repeated("s_n1d", MT)
        s_s = Repeated("s_scores", UNITS)
        s_nm = Repeated("s_negmax", UNITS)
        s_p = Repeated("s_probs", UNITS)
        s_t = Repeated("s_probsT", UNITS)
        s_ta = Repeated("s_pTa", UNITS)
        s_td = Repeated("s_pTd", wide(0, UNITS))
        s_o = Repeated("s_pv", UNITS)
        s_oe = Repeated("s_oevac", UNITS)
        s_or = Repeated("s_orow", UNITS // 2)
        s_ovar = Repeated("s_ovar", 4 * MT)
        s_orstd = Repeated("s_orstd", 4 * MT)
        s_x = Repeated("s_mixT", UNITS // 2)
        s_xe = Repeated("s_mixed", UNITS // 2)
        s_op = Repeated("s_outproj", 2 * MT)
        s_oped = Repeated("s_outevac", 2 * MT)
        s_xup = Repeated("s_xup", MT)
        s_n2ss = Repeated("s_n2ss", MT)
        s_n2var = Repeated("s_n2var", MT)
        s_n2r = Repeated("s_n2r", MT)
        s_h2 = Repeated("s_h2", MT)
        s_n2t = Repeated("s_n2t", MT)
        s_n2a = Repeated("s_n2a", MT)
        s_n2d = Repeated("s_n2d", MT)
        s_h2st = [Repeated(f"s_h2st{b}", 16 * (3 - b)) for b in range(2)]
        s_rt = Repeated("s_router", MT)
        s_rx = Repeated("s_rexp", MT)
        s_mask = Repeated("s_mask", 1)
        s_cnt = Repeated("s_count", 1)
        s_slots = Repeated("s_slots", 1)
        s_scat = Repeated("s_scatter", 32 * MT)
        s_idl = Repeated("s_idload", 16)
        s_idt = Repeated("s_idT", 1)
        s_ids = Repeated("s_ids", 1)
        ld_wswa, ld_scache, zeroed, ld_fg = (sem(n) for n in ("ld_wswa", "ld_scache", "zeroed", "ld_fg"))
        s_filled = sem("s_filled")
        s_adaev, s_adatr = sem("s_adaev"), sem("s_adatr")
        s_cexp, s_csil, s_adamm, s_adac, s_adat, s_adar, s_adast, s_adat2, s_adacol = (
            sem(n) for n in ("s_cexp", "s_csil", "s_adamm", "s_adac", "s_adat", "s_adar", "s_adast", "s_adat2", "s_adacol"))
        s_lamx, s_lamp = sem("s_lamx"), sem("s_lamp")
        s_abp, s_aba, s_abd, s_abss, s_abvar, s_abr, s_abrow, s_abt, s_abta, s_abtd, s_about = (
            sem(n) for n in ("s_abp", "s_aba", "s_abd", "s_abss", "s_abvar", "s_abr", "s_abrow", "s_abt", "s_abta",
                             "s_abtd", "s_about"))
        s_qbp, s_qba, s_qbr, s_qbt, s_qbta, s_qbtd = (
            sem(n) for n in ("s_qbp", "s_qba", "s_qbr", "s_qbt", "s_qbta", "s_qbtd"))
        s_kvp, s_kva, s_kvd, s_krc = (sem(n) for n in ("s_kvp", "s_kva", "s_kvd", "s_krc"))
        s_swp, s_swd, s_swrow, s_swt, s_swta, s_swtd, s_swout = (
            sem(n) for n in ("s_swp", "s_swd", "s_swrow", "s_swt", "s_swta", "s_swtd", "s_swout"))
        s_mt, s_gu, s_dn, s_xea, s_xed, s_ex, s_mc, s_act, s_yea, s_yed, s_idc, s_comb = (
            per_layer(n) for n in ("s_moeT", "s_gateup", "s_down", "s_xTa", "s_xTd", "s_moeexp", "s_moechain",
                                   "s_moeact", "s_yea", "s_yed", "s_idcopy", "s_combined"))
        s_xg = [[sem(f"s_xg{b}_l{l}") for b in range(2)] for l in range(2)]
        s_wgu = [[sem(f"s_wgu{b}_l{l}") for b in range(2)] for l in range(2)]
        s_wd = [[sem(f"s_wd{b}_l{l}") for b in range(2)] for l in range(2)]
        s_yw = [[sem(f"s_yw{b}_l{l}") for b in range(2)] for l in range(2)]
        s_yc = [Repeated(f"s_yc{m}", 32) for m in range(MT)]
        s_fss, s_fvar, s_fr, s_fy, s_fout = (sem(n) for n in ("s_fss", "s_fvar", "s_fr", "s_fy", "s_fout"))
        chain_d = sem("dve_chain")
        s_idseen = sem("s_idseen")

        NP = NT // 2
        assert NT % 2 == 1
        AB_ORDER = [3, 4, 0, 1, 2]
        AB_COLS = [(0, 512), (512, 512), (1024, 512), (1536, QL), (1536 + QL, CKV + KR)]
        scale_of = {"diff": 64 ** -0.5, "mla": MQ ** -0.5, "swa": 64 ** -0.5}

        def cond(m):
            return 1 if m == PROMPT else 0

        def acolumn(l, m, j, k):
            at = cond(m) * 48 + j * 8 + k
            return ada_cols[l][:, at:at + 1]

        def tile_of(ap, m):
            return ap[:, m * P:(m + 1) * P]

        def q_of(l, u):
            kind, m, h, _ = u
            half = slice((h % 2) * 64, (h % 2) * 64 + 64)
            if kind == "mla":
                return qbT[0:MQ, h, m * P:(m + 1) * P]
            return (qaT if kind == "diff" else qsT)[half, h // 2, m * P:(m + 1) * P]

        def k_of(l, u, kt, n):
            kind, m, h, _ = u
            half = slice((h % 2) * 64, (h % 2) * 64 + 64)
            cols = slice(kt * P, (kt + n) * P)
            if kind == "mla":
                return kbT[0:MQ, h, cols]
            return kaT[half, h // 2, cols] if kind == "diff" else ksT[half, h // 4, cols]

        def v_of(l, u, kt):
            kind, m, h, _ = u
            if kind == "diff":
                return vd[:, kt, (h // 2) * P:(h // 2 + 1) * P]
            return vb[:, kt, h * 64:(h + 1) * 64] if kind == "mla" else vs[:, kt, (h // 4) * 64:(h // 4 + 1) * 64]

        def v_width(u):
            return P if u[0] == "diff" else 64

        def row_bc(ap):
            return ap.to_broadcast([P, ap.shape[-1]])

        ada_src = ada_w.rearrange("l (p k) n -> l p k n", k=KC)
        kp = "(k p) n -> p k n"

        block = ctx.enter_context(nc.Block())

        @block.sync
        def _(sp):
            sp.dma_start(cst[:], consts).then_inc(ld_cst, 16)
            sp.dma_start(cin[:, 0, :], c_s.rearrange("a (p k) -> p (a k)", k=KC)).then_inc(ld_c, 16)
            sp.dma_start(cin[:, 1, :], c_ctx.rearrange("(p k) -> p k", k=KC)).then_inc(ld_c, 16)
            sp.dma_start(x_rows[:, 0:4, :], x_sample.rearrange("a (m p) d -> p (a m) d", p=P)).then_inc(ld_x, 16)
            sp.dma_start(x_rows[:, 4, :], x_prompt.rearrange("a p d -> p (a d)")).then_inc(ld_x, 16)

            def ada_addends(l):
                for q in range(2):
                    sp.dma_start(radd[l][48 * q:48 * q + 48, :], ada_b[l].rearrange("(j p) -> j p", p=P)).then_inc(ld_mod, 16)
                    for j, n, g in ((0, 1, None), (1, 1, norm1_g), (2, 2, None), (4, 1, norm2_g), (5, 1, None)):
                        at = 48 * q + 8 * j
                        src = consts[0:8 * n, C_ONE:C_ONE + P] if g is None else g[l].rearrange("(j p) -> j p", p=P)
                        sp.dma_start(rmul[l][at:at + 8 * n, :], src).then_inc(ld_mod, 16)

            def ada_weights(l, first, end):
                for i in range(12 * l + first, 12 * l + end):
                    if i >= 3:
                        sp.wait_ge(s_adamm, i - 2)
                    sp.dma_start(ada_ring[l][i % 3], ada_src[l][:, :, (i - 12 * l) * 512:(i - 12 * l + 1) * 512])\
                        .then_inc(ld_ada[i % 3], 16)

            ada_weights(0, 0, 3)
            ada_addends(0)
            ada_weights(0, 3, 12)
            sp.wait_ge(s_adamm, 12)
            sp.dma_start(wqb, mla_w_qb[0].rearrange(kp, p=P)).then_inc(ld_lat, 16)
            for k in range(2):
                for t in range(2):
                    sp.dma_start(wkvb[:, k, t * 512:(t + 1) * 512].rearrange("p (h d) -> p h d", d=64),
                                 mla_w_kvb[0, k * P:(k + 1) * P, :].rearrange("p (h t d) -> p h t d", t=2, d=64)[:, :, t, :])\
                        .then_inc(ld_lat, 16)
            sp.wait_ge(s_n1t.sem, s_n1t.at(0, MT))
            sp.dma_start(vd[:, CACHE_KT, :], cache_diff_v.rearrange("a b s h d -> s (a b h d)")).then_inc(ld_vcache, 16)
            sp.wait_ge(s_adar, 1)
            sp.dma_start(ada_rows[0].rearrange("q (j p) -> (q j) p", p=P), arow[0][0:96, :]).then_inc(s_adast, 16)
            sp.wait_ge(s_adast, 16)

            def load_rows(dst, l, j, s):
                for q in range(2):
                    sp.dma_start(dst[q], row_bc(ada_rows[l, q:q + 1, j * D:(j + 1) * D])).then_inc(s, 16)

            load_rows(gate, 0, 2, ld_gate.sem)
            sp.wait_ge(s_abrow, MT)
            sp.wait_ge(s_aba, 3 * MT)
            sp.wait_ge(s_abd, 2 * MT)
            sp.dma_start(new_diff_k.rearrange("a b s h t d -> s (a b h t d)"), krow).then_inc(s_about, 16)
            sp.dma_start(new_diff_v.rearrange("a b s h d -> s (a b h d)"), vd[:, PROMPT_KT, :]).then_inc(s_about, 16)
            sp.dma_start(new_mla_ckv.rearrange("a b s d -> s (a b d)"), cvrow[:, 0:CKV]).then_inc(s_about, 16)
            sp.dma_start(new_mla_krope.rearrange("a b s d -> s (a b d)"), cvrow[:, CKV:]).then_inc(s_about, 16)
            sp.wait_ge(s_kvp, 14)
            sp.wait_ge(s_krc, 8)
            sp.dma_start(w_abo, ab_w_out[0].rearrange(kp, p=P)).then_inc(ld_wout.sem, 16)
            sp.wait_ge(s_about, 64)
            sp.wait_ge(s_o.sem, s_o.at(0, 8 * MT))
            sp.dma_start(x_rows[:, 0:4, :], x_sample.rearrange("a (m p) d -> p (a m) d", p=P)).then_inc(ld_x2, 16)
            sp.dma_start(x_rows[:, 4, :], x_prompt.rearrange("a p d -> p (a d)")).then_inc(ld_x2, 16)

            for l in range(2):
                if l == 0:
                    for w, j in enumerate((4, 3)):
                        load_rows([bc[0][:, 2 * w, :], bc[0][:, 2 * w + 1, :]], 0, j, ld_bc.sem)
                    sp.wait_ge(s_s.sem, s_s.at(0, len(units[0])))
                    sp.wait_ge(s_o.sem, s_o.at(0, len(units[0])))
                    ada_weights(1, 0, 3)
                    ada_addends(1)
                else:
                    sp.wait_ge(s_comb[0], MT)
                    sp.dma_start(w_swao, swa_w_out[0].rearrange(kp, p=P)).then_inc(ld_wout.sem, 16)
                    for t in range(2):
                        sp.dma_start(cache_k.rearrange("p (h t d) -> p h t d", t=2, d=64)[:, :, t, :],
                                     cache_swa_k.rearrange("a b s h d -> s (a b h) d")).then_inc(ld_scache, 16)
                    sp.dma_start(vs[:, CACHE_KT, :], cache_swa_v.rearrange("a b s h d -> s (a b h d)")).then_inc(ld_scache, 16)
                    sp.wait_ge(s_n1t.sem, s_n1t.at(1, MT))
                    sp.wait_ge(s_adast, 32)
                    load_rows(gate, 1, 2, ld_gate.sem)
                    sp.wait_ge(s_swrow, MT)
                    sp.dma_start(new_swa_k.rearrange("a b s h d -> s (a b h) d"), ksrow[:, :, 0, :]).then_inc(s_swout, 16)
                    sp.dma_start(new_swa_v.rearrange("a b s h d -> s (a b h d)"), vs[:, PROMPT_KT, :]).then_inc(s_swout, 16)
                    sp.wait_ge(s_swp, 3 * MT)
                    for w, j in enumerate((4, 3)):
                        load_rows([bc[1][:, 2 * w, :], bc[1][:, 2 * w + 1, :]], 1, j, ld_bc.sem)
                    sp.wait_ge(s_swout, 32)
                for m in range(MT):
                    sp.wait_ge(s_h2.sem, s_h2.at(l, m + 1))
                    sp.dma_start(h2_dram[m * P:(m + 1) * P, :], xg[l][m % 2]).then_inc(s_h2st[m % 2].sem, 16)
                load_rows(gate, l, 5, ld_gate2.sem)
                if l == 0:
                    ada_weights(1, 3, 12)
                sp.wait_ge(s_slots.sem, s_slots.at(l, 1))
                sp.wait_ge(s_op.sem, s_op.at(l, 2 * MT))

                def expert_of(t):
                    return sp.value_load(eidi[0:1, bass.ds(t, 1)], min_val=0, max_val=E - 1)

                def weights(e, b, down):
                    todo = ((wd[b], moe_w_down),) if down else ((wg[b], moe_w_gate), (wu[b], moe_w_up))
                    for dst, src in todo:
                        sp.dma_start(dst, src[l][bass.ds(e, 1), :, :].rearrange("e (k p) n -> p (e k) n", p=P))\
                            .then_inc((s_wd if down else s_wgu)[l][b], 16)

                def expert_rows_out(i, b):
                    t = 2 * i + b
                    sp.wait_ge(s_yea[l], t + 3)
                    sp.wait_ge(s_yed[l], t + 3)
                    sp.dma_start(y_dram[bass.ds(t * P, P), :], yr[b]).then_inc(s_yw[l][b], 16)

                sp.wait_ge(s_ids.sem, s_ids.at(l, 1))
                for b in range(2):
                    e = expert_of(b)
                    weights(e, b, False)
                    weights(e, b, True)

                def next_weights(i, b):
                    e = expert_of(2 * i + 2 + b)
                    sp.wait_ge(s_gu[l], 2 * i + b + 1)
                    weights(e, b, False)
                    sp.wait_ge(s_dn[l], 2 * i + b + 1)
                    weights(e, b, True)

                if l == 0:
                    sp.wait_ge(s_adamm, 24)
                    sp.dma_start(w_swa, swa_w_in[0].rearrange(kp, p=P)).then_inc(ld_wswa, 16)
                    sp.wait_ge(s_adar, 2)
                    sp.dma_start(ada_rows[1].rearrange("q (j p) -> (q j) p", p=P), arow[1][0:96, :]).then_inc(s_adast, 16)
                with sp.Fori(0, NP - 1) as i:
                    for b in range(2):
                        next_weights(i, b)
                        expert_rows_out(i, b)
                next_weights(NP - 1, 0)
                for b in range(2):
                    expert_rows_out(NP - 1, b)
                expert_rows_out(NP, 0)

            sp.wait_ge(s_swp, 3 * MT)
            sp.wait_ge(s_n2d.sem, s_n2d.at(1, MT))
            sp.wait_ge(s_h2.sem, s_h2.at(1, MT))
            sp.dma_start(bc[1][:, 0, :], row_bc(final_norm_g.rearrange("(a d) -> a d", a=1))).then_inc(ld_fg, 16)
            for m in range(MT):
                sp.wait_ge(s_fy, m + 1)
                dst = y_prompt.rearrange("a p d -> (a p) d") if m == PROMPT else \
                    y_sample.rearrange("a p d -> (a p) d")[m * P:(m + 1) * P, :]
                sp.dma_start(dst, x_rows[:, m, :]).then_inc(s_fout, 16)
            sp.wait_ge(s_fout, 16 * MT)

        @block.scalar
        def _(act):
            for q in range(4):
                act.dma_start(w_in[:, 2 * q:2 * q + 2, :], ab_w_in[0].rearrange(kp, p=P)[:, 2 * q:2 * q + 2, :])\
                    .then_inc(ld_win, 16)
            act.dma_start(sqj[:, 0:256], row_bc(diff_lambda.rearrange("l a d -> l (a d)"))).then_inc(ld_small, 16)
            act.dma_start(ckv_g[:], row_bc(mla_kv_norm_g)).then_inc(ld_small, 16)
            for k in range(3):
                act.dma_start(gcols[:, k:k + 1], mla_q_norm_g[0:1, k * P:(k + 1) * P].rearrange("a p -> p a"))\
                    .then_inc(ld_small, 16)
            act.dma_start(gcols[:, 3:4], diff_subln_g.rearrange("a p -> p a")).then_inc(ld_small, 16)
            act.dma_start(rw[:], router_w.rearrange("(k p) e -> p k e", p=P)).then_inc(ld_small, 16)
            act.dma_start(rbias[:], row_bc(router_bias.rearrange("(a e) -> a e", a=1))).then_inc(ld_small, 16)
            act.dma_start(sink8[:], row_bc(swa_sink)).then_inc(ld_small, 16)
            act.dma_start(cache_k[:], cache_diff_k.rearrange("a b s h t d -> s (a b h t d)")).then_inc(ld_cache, 16)
            act.dma_start(cache_c[:, 0:CKV], cache_mla_ckv.rearrange("a b s d -> s (a b d)")).then_inc(ld_cache, 16)
            act.dma_start(cache_c[:, CKV:], cache_mla_krope.rearrange("a b s d -> s (a b d)")).then_inc(ld_cache, 16)
            act.wait_ge(ld_c, 32)
            nc.scalar.activation(cex[:], cin[:], ACT.Exp, scale=-1.0).then_inc(s_cexp, 1)
            act.wait_ge(s_lamp, 1)
            nc.scalar.activation(lam[:, 2:4], lam[:, 0:2], ACT.Exp).then_inc(s_lamx, 1)

            def square_sums(l):
                for m in range(MT):
                    if m:
                        act.wait_ge(s_ss.sem, s_ss.at(l, m))
                    nc.scalar.activation(junk, x_rows[:, m, :], ACT.Square, accum_out=ss[:, m:m + 1]).then_inc(s_ss.sem, 1)

            def norm1_evac(l):
                for m in range(MT):
                    act.wait_ge(s_n1t.sem, s_n1t.at(l, m + 1))
                    for k in range(4):
                        ins = nc.scalar.activation(hT[:, k, m * P:(m + 1) * P], ps[:, (m % 2) * 2, k * P:(k + 1) * P],
                                                   ACT.Identity, scale=acolumn(l, m, 1, k), bias=acolumn(l, m, 0, k))
                    ins.then_inc(s_n1a.sem, 1)

            act.wait_ge(ld_x, 32)
            square_sums(0)

            def ada_rows_out(l):
                for i in range(12 * l, 12 * l + 12):
                    act.wait_ge(s_adamm, i + 1)
                    if i >= 2:
                        act.wait_ge(s_adatr, i - 1)
                    nc.scalar.activation(ada_out[l][i % 2][0:2, :], ps[0:2, 4 + i % 2, :], ACT.Copy).then_inc(s_adaev, 1)

            ada_rows_out(0)
            act.wait_ge(s_adacol, 1)
            norm1_evac(0)

            act.wait_ge(ld_small, 9 * 16)

            def ab_transposed(m):
                act.wait_ge(s_abt, 4 * m + 2)
                kt = PROMPT_KT if m == PROMPT else m
                nc.scalar.activation(kaT[:, :, kt * P:(kt + 1) * P], ps[:, 1, :].rearrange("p (c t) -> p c t", c=4),
                                     ACT.Copy).then_inc(s_abta, 1)
                act.wait_ge(s_abt, 4 * m + 3)
                for k in range(3):
                    ins = nc.scalar.activation(qlT[:, k, m * P:(m + 1) * P], ps[:, 2, k * P:(k + 1) * P], ACT.Copy,
                                               scale=gcols[:, k:k + 1])
                ins.then_inc(s_abta, 1)

            for m in range(MT):
                n = 5 * m
                act.wait_ge(s_abp, n + 1)
                if m:
                    act.wait_ge(s_abss, 2 * m)
                nc.scalar.activation(sqj[:, 0:QL], ps[:, 4 + n % 4, 0:QL], ACT.Square, accum_out=ss[:, 8:9])\
                    .then_inc(s_abss, 1)
                act.wait_ge(s_abp, n + 2)
                act.wait_ge(s_abss, 2 * m + 1)
                nc.scalar.activation(sqj[:, 0:CKV], ps[:, 4 + (n + 1) % 4, 0:CKV], ACT.Square, accum_out=ss[:, 9:10])\
                    .then_inc(s_abss, 1)
                if m:
                    ab_transposed(m - 1)
                    act.wait_ge(s_abt, 4 * m)
                act.wait_ge(s_abr, m + 1)
                nc.scalar.activation(qlrow, ps[:, 4 + n % 4, 0:QL], ACT.Copy, scale=rstd[:, 8:9]).then_inc(s_aba, 1)
                nc.scalar.activation(cvrow[:, 0:CKV], ps[:, 4 + (n + 1) % 4, 0:CKV], ACT.Copy, scale=rstd[:, 9:10])
                nc.scalar.activation(cvrow[:, CKV:], ps[:, 4 + (n + 1) % 4, CKV:CKV + KR], ACT.Copy).then_inc(s_aba, 1)
                act.wait_ge(s_abp, n + 5)
                kt = PROMPT_KT if m == PROMPT else m
                nc.scalar.activation(vd[:, kt, :], ps[:, 4 + (n + 4) % 4, :], ACT.Copy).then_inc(s_aba, 1)
            ab_transposed(MT - 1)
            act.wait_ge(s_abt, 4 * MT + 1)
            nc.scalar.activation(kaT[:, :, CACHE_KT * P:(CACHE_KT + 1) * P], ps[:, 1, :].rearrange("p (c t) -> p c t", c=4),
                                 ACT.Copy).then_inc(s_abta, 1)

            act.wait_ge(s_about, 64)
            act.wait_ge(s_abt, 4 * MT + 2)

            def qb_transposed(m):
                act.wait_ge(s_qbt, 2 * m + 2)
                nc.scalar.activation(qbT[0:MQ, 4:8, m * P:(m + 1) * P],
                                     ps[0:MQ, (m % 2) * 2 + 1, :].rearrange("p (c t) -> p c t", c=4), ACT.Copy)\
                    .then_inc(s_qbta, 1)

            for j in range(2 * MT):
                m, half = divmod(j, 2)
                if m >= 2 and half == 0:
                    act.wait_ge(s_qbt, 2 * (m - 1))
                act.wait_ge(s_qbp, j + 1)
                nc.scalar.activation(qbrow[m % 2][:, half * 384:(half + 1) * 384], ps[:, 4 + j % 4, 0:384], ACT.Copy)\
                    .then_inc(s_qba, 1)
                if half and m:
                    qb_transposed(m - 1)
            qb_transposed(MT - 1)
            for kt in range(KT):
                act.wait_ge(s_kvp, 2 * kt + 1)
                nc.scalar.activation(vb[:, kt, :], ps[:, 4 + (2 * kt) % 4, :], ACT.Copy).then_inc(s_kva, 1)

            def attention(l):
                U = units[l]
                n = len(U)
                for i in range(n + 5):
                    if i < n:
                        kind, m, h, kts = U[i]
                        w = len(kts) * P + (kind == "swa")
                        act.wait_ge(s_nm.sem, s_nm.at(l, i + 1))
                        if i >= 2:
                            act.wait_ge(s_t.sem, s_t.at(l, i - 1))
                        sc = ps[:, 2 * (i % 2):2 * (i % 2) + 2, :].rearrange("p a b -> p (a b)")[:, 0:w]
                        nc.scalar.activation(prow[i % 2][:, 0:w], sc, ACT.Exp, bias=nmx[:, i % 4:i % 4 + 1],
                                             scale=scale_of[kind], accum_out=rsum[:, i % 4:i % 4 + 1])\
                            .then_inc(s_p.sem, 1)
                    if 1 <= i <= n:
                        kts = U[i - 1][3]
                        w = min(len(kts), 4)
                        act.wait_ge(s_t.sem, s_t.at(l, i))
                        nc.scalar.activation(pT[(i - 1) % 2][:, 0:w, :],
                                             ps[:, 4, 0:w * P].rearrange("p (c t) -> p c t", c=w), ACT.Copy)\
                            .then_inc(s_ta.sem, 1)
                    if i >= 5 and i % 2:
                        j = (i - 5) // 2
                        kind, m, h, _ = U[2 * j]
                        chunk = h // 2 + (4 if kind == "mla" else 0)
                        act.wait_ge(s_x.sem, s_x.at(l, j + 1))
                        dst = hT[:, chunk, m * P:(m + 1) * P]
                        if kind == "diff":
                            ins = nc.scalar.activation(dst, ps[:, 7, 0:P], ACT.Copy, scale=lam[:, 5:6])
                        else:
                            ins = nc.scalar.activation(dst, ps[:, 7, 0:P], ACT.Copy)
                        ins.then_inc(s_xe.sem, 1)

            def norm2(l):
                for m in range(MT + 3):
                    if m < MT:
                        act.wait_ge(s_xup.sem, s_xup.at(l, m + 1))
                        if m:
                            act.wait_ge(s_n2ss.sem, s_n2ss.at(l, m))
                        nc.scalar.activation(junk, x_rows[:, m, :], ACT.Square, accum_out=ss[:, m:m + 1])\
                            .then_inc(s_n2ss.sem, 1)
                    if 2 <= m <= MT + 1:
                        act.wait_ge(s_n2t.sem, s_n2t.at(l, m - 1))
                        nc.scalar.activation(xgT[l][m % 2][:, 0:4, :],
                                             ps[:, 4, :].rearrange("p (c t) -> p c t", c=4), ACT.Copy)\
                            .then_inc(s_n2a.sem, 1)
                    if m >= 3:
                        act.wait_ge(s_rt.sem, s_rt.at(l, m - 2))
                        nc.scalar.activation(scores[:, m - 3, :], ps[:, 6, 0:E], ACT.Exp, scale=-1.0)\
                            .then_inc(s_rx.sem, 1)

            def experts(l):
                def gathered(i, b):
                    t = 2 * i + b
                    act.wait_ge(s_mt[l], t + 1)
                    nc.scalar.activation(xgT[l][b][:, 0:4, :], ps[:, 0, :].rearrange("p (c t) -> p c t", c=4),
                                         ACT.Copy).then_inc(s_xea[l], 1)
                    act.wait_ge(s_gu[l], t + 1)
                    nc.scalar.activation(ebuf[b], ps[:, 2 + b, 0:2 * P], ACT.Exp, scale=-1.0).then_inc(s_ex[l], 1)

                def out_rows(i, b):
                    act.wait_ge(s_dn[l], 2 * i + b + 1)
                    act.wait_ge(s_yw[l][b], 16 * i + 16)
                    nc.scalar.activation(yr[b][:, 0:512], ps[:, 4 + 2 * b, :], ACT.Copy).then_inc(s_yea[l], 1)

                for b in range(2):
                    act.sem_inc(s_yw[l][b], 16)
                act.sem_inc(s_yea[l], 2)
                gathered(0, 0)
                with act.Fori(0, NP) as i:
                    gathered(i, 1)
                    out_rows(i, 0)
                    gathered(i + 1, 0)
                    out_rows(i, 1)
                out_rows(NP, 0)

            attention(0)
            act.wait_ge(s_t.sem, s_t.at(0, len(units[0])))
            act.wait_ge(s_o.sem, s_o.at(0, len(units[0])))
            norm2(0)
            ada_rows_out(1)
            experts(0)
            act.wait_ge(s_comb[0], MT)
            square_sums(1)
            norm1_evac(1)

            def sw_transposed(m, kt):
                if kt != CACHE_KT:
                    act.wait_ge(s_swt, 3 * m + 1)
                    nc.scalar.activation(qsT[:, 0:4, m * P:(m + 1) * P], ps[:, 0, :].rearrange("p (c t) -> p c t", c=4),
                                         ACT.Copy).then_inc(s_swta, 1)
                    act.wait_ge(s_swt, 3 * m + 3)
                else:
                    act.wait_ge(s_swt, 3 * MT + 1)
                nc.scalar.activation(ksT[:, :, kt * P:(kt + 1) * P], ps[:, 2, :].rearrange("p (c t) -> p c t", c=4),
                                     ACT.Copy).then_inc(s_swta, 1)

            for m in range(MT):
                sw_transposed(m, PROMPT_KT if m == PROMPT else m)
            sw_transposed(MT, CACHE_KT)
            act.wait_ge(s_swout, 32)
            act.wait_ge(s_swt, 3 * MT + 1)
            attention(1)
            act.wait_ge(s_t.sem, s_t.at(1, len(units[1])))
            act.wait_ge(s_o.sem, s_o.at(1, len(units[1])))
            norm2(1)
            experts(1)
            for m in range(MT):
                act.wait_ge(s_comb[1], m + 1)
                if m:
                    act.wait_ge(s_fss, m)
                nc.scalar.activation(junk, x_rows[:, m, :], ACT.Square, accum_out=ss[:, m:m + 1]).then_inc(s_fss, 1)

        @block.gpsimd
        def _(pool):
            nc.gpsimd.memset(mhalf[:], -0.5).then_inc(s_filled, 1)
            nc.gpsimd.memset(idrow[0:NT, :], 0.0).then_inc(s_filled, 1)
            pool.wait_ge(s_filled, 2)
            pool.dma_start(slot_dram.rearrange("(t p) o -> t (p o)", p=P), idrow[0:NT, :]).then_inc(zeroed, 16)
            pool.wait_ge(zeroed, 16)

            def inverse_root(at, n, ready, value, done):
                pool.wait_ge(ready, value)
                nc.gpsimd.tensor_tensor(rstd[:, at:at + n], var[:, at:at + n], mhalf[:, at:at + n], ALU.pow)\
                    .then_inc(done, 1)

            def head_roots():
                for j in range(4 * MT):
                    inverse_root(12 + j % 2, 1, s_ovar.sem, j + 1, s_orstd.sem)

            def after_attention(l):
                for m in range(MT):
                    inverse_root(m, 1, s_n2var.sem, s_n2var.at(l, m + 1), s_n2r.sem)
                pool.wait_ge(s_slots.sem, s_slots.at(l, 1))
                for w in range(2):
                    for m in range(MT):
                        pool.indirect_dma_start(slot_dram, bass.IndirectOffsetOnAxis(slots[:, w, m:m + 1], 0),
                                                cst[:, C_TOK + m:C_TOK + m + 1], None).then_inc(s_scat.sem, 16)
                pool.wait_ge(s_scat.sem, s_scat.at(l, 160))
                pool.dma_start(idrow[0:NT, :], slot_dram.rearrange("(t p) o -> t (p o)", p=P)).then_inc(s_idl.sem, 16)
                pool.wait_ge(s_ids.sem, s_ids.at(l, 1))
                for b in range(2):
                    pool.wait_ge(s_h2st[b].sem, s_h2st[b].at(l, 16 * (3 - b)))

                def gather(t, b, n):
                    nc.gpsimd.tensor_copy(idt[b][:], idall[:, bass.ds(t, 1)]).then_inc(s_idc[l], 1)
                    pool.wait_ge(s_idc[l], n)
                    pool.sem_inc(s_idseen, 1)
                    pool.indirect_dma_start(xg[l][b], None, h2_dram, bass.IndirectOffsetOnAxis(idt[b][:], 0))\
                        .then_inc(s_xg[l][b], 16)

                for b in range(2):
                    gather(b, b, b + 1)
                with pool.Fori(0, NP - 1) as i:
                    for b in range(2):
                        pool.wait_ge(s_mt[l], 2 * i + b + 1)
                        gather(2 * i + 2 + b, b, 2 * i + 3 + b)
                pool.wait_ge(s_mt[l], NT - 2)
                gather(NT - 1, 0, NT)
                for b in range(2):
                    pool.wait_ge(s_yw[l][b], 16 * (NP + 2 - b))
                for m in range(MT):
                    for w in range(2):
                        pool.indirect_dma_start(yc[2 * m + w], None, y_dram,
                                                bass.IndirectOffsetOnAxis(slots[:, w, m:m + 1], 0))\
                            .then_inc(s_yc[m].sem, 16)

            inverse_root(0, MT, s_var.sem, s_var.at(0, 1), s_rstd.sem)
            for m in range(MT):
                inverse_root(8, 2, s_abvar, m + 1, s_abr)
            pool.wait_ge(s_abtd, 2 * MT + 1)
            pool.wait_ge(s_abp, 5 * MT)
            for h in range(MH):
                nc.gpsimd.tensor_copy(kbT[64:96, h, :], krT[0:32, :]).then_inc(s_krc, 1)
            head_roots()
            after_attention(0)
            inverse_root(0, MT, s_var.sem, s_var.at(1, 1), s_rstd.sem)
            after_attention(1)
            for m in range(MT):
                inverse_root(m, 1, s_fvar, m + 1, s_fr)

        @block.vector
        def _(dve):
            steps = [0]

            def link(*instructions):
                for ins in instructions:
                    ins.then_inc(chain_d, 1)
                    steps[0] += 1
                dve.wait_ge(chain_d, steps[0])

            tt = nc.vector.tensor_tensor
            ts = nc.vector.tensor_scalar

            dve.wait_ge(s_cexp, 1)
            link(ts(cex[:], cex[:], 1.0, None, ALU.add))
            link(nc.vector.reciprocal(cex[:], cex[:]))
            tt(csil[:], cin[:], cex[:], ALU.mult).then_inc(s_csil, 1)
            dve.wait_ge(ld_small, 9 * 16)
            l4 = sqj[:, 0:256].rearrange("p (a b d) -> p a b d", a=2, b=2)
            link(tt(sqj[:, 256:384].rearrange("p (a d) -> p a d", a=2), l4[:, :, 0, :], l4[:, :, 1, :], ALU.mult))
            nc.vector.tensor_reduce(lam[:, 0:2], sqj[:, 256:384].rearrange("p (a d) -> p a d", a=2), AX_X, ALU.add)\
                .then_inc(s_lamp, 1)
            dve.wait_ge(s_lamx, 1)
            link(tt(lam[:, 4:5], lam[:, 3:4], lam[:, 2:3], ALU.subtract))
            link(ts(lam[:, 4:5], lam[:, 4:5], -LAMBDA_INIT, None, ALU.add))
            link(ts(lam[:, 5:6], gcols[:, 3:4], 1.0 - LAMBDA_INIT, None, ALU.mult))
            link(ts(sink8[:], sink8[:], 8.0, None, ALU.mult))

            def variance(at, n, width, *, out):
                ts(var[:, at:at + n], ss[:, at:at + n], 1.0 / width, EPS, ALU.mult, ALU.add).then_inc(out, 1)

            dve.wait_ge(s_ss.sem, s_ss.at(0, MT))
            variance(0, MT, D, out=s_var.sem)

            def ada(l):
                dve.wait_ge(s_adatr, 12 * (l + 1))
                nc.vector.tensor_copy(acol[l], ps[:, l, 0:96]).then_inc(s_adac, 1)
                dve.wait_ge(s_adat, l + 1)
                dve.wait_ge(ld_mod, 12 * 16 * (l + 1))
                dve.wait_ge(ld_cst, 16)
                link(nc.vector.scalar_tensor_tensor(out=arow[l][0:96, :], in0=ps[0:96, 2 + l, 0:P],
                                                    scalar=cst[0:96, C_SCL:C_SCL + 1], in1=radd[l][0:96, :],
                                                    op0=ALU.add, op1=ALU.add))
                tt(arow[l][0:96, :], arow[l][0:96, :], rmul[l][0:96, :], ALU.mult).then_inc(s_adar, 1)
                dve.wait_ge(s_adat2, l + 1)
                nc.vector.tensor_copy(ada_cols[l][:], ps[:, 4 + l, 0:96]).then_inc(s_adacol, 1)

            def normed(l, m):
                if m >= 2:
                    dve.wait_ge(s_n1t.sem, s_n1t.at(l, m - 1))
                ts(xn[m % 2], x_rows[:, m, :], rstd[:, m:m + 1], None, ALU.mult).then_inc(s_xn.sem, 1)

            def norm1(l):
                for m in range(MT + 1):
                    if m < MT:
                        normed(l, m)
                    if m:
                        dve.wait_ge(s_n1t.sem, s_n1t.at(l, m))
                        for k in range(4, KC):
                            ins = ts(hT[:, k, (m - 1) * P:m * P], ps[:, ((m - 1) % 2) * 2 + 1, (k - 4) * P:(k - 3) * P],
                                     acolumn(l, m - 1, 1, k), acolumn(l, m - 1, 0, k), ALU.mult, ALU.add)
                        ins.then_inc(s_n1d.sem, 1)

            ada(0)
            dve.wait_ge(s_rstd.sem, s_rstd.at(0, 1))
            norm1(0)
            dve.wait_ge(s_adast, 16)

            def rope(dst, src, m, dim, heads, done=None):
                def tab(c):
                    return cst[:, c + m * dim:c + (m + 1) * dim].unsqueeze(1).broadcast_to([P, heads, dim])
                co, si = tab(C_C64 if dim == 64 else C_C32), tab(C_S64 if dim == 64 else C_S32)
                n = heads * dim
                t = rtmp[:, 0:n].rearrange("p (h d) -> p h d", h=heads)
                t2 = rtmp2[:, 0:n].rearrange("p (h d) -> p h d", h=heads)
                link(tt(t, src, co, ALU.mult),
                     tt(t2[:, :, 0::2], src[:, :, 1::2], si[:, :, 0::2], ALU.mult),
                     tt(t2[:, :, 1::2], src[:, :, 0::2], si[:, :, 1::2], ALU.mult))
                return tt(dst, t, t2, ALU.add)

            def ab_transposed(m):
                dve.wait_ge(s_abt, 4 * m + 1)
                nc.vector.tensor_copy(qaT[:, :, m * P:(m + 1) * P], ps[:, 0, :].rearrange("p (c t) -> p c t", c=4))
                latents_transposed(PROMPT_KT if m == PROMPT else m, 4 * m + 4)

            def latents_transposed(kt, n):
                dve.wait_ge(s_abt, n)
                nc.vector.tensor_copy(ckvT[:, :, kt * P:(kt + 1) * P], ps[:, 3, 0:2 * P].rearrange("p (c t) -> p c t", c=2))
                nc.vector.tensor_copy(krT[0:KR, kt * P:(kt + 1) * P], ps[0:KR, 3, 2 * P:3 * P]).then_inc(s_abtd, 2 if n % 4 == 0 else 1)

            for m in range(MT):
                n = 5 * m
                dve.wait_ge(s_abss, 2 * m + 2)
                ts(var[:, 8:9], ss[:, 8:9], 1.0 / QL, EPS, ALU.mult, ALU.add)
                ts(var[:, 9:10], ss[:, 9:10], 1.0 / CKV, EPS, ALU.mult, ALU.add).then_inc(s_abvar, 1)
                if m:
                    ab_transposed(m - 1)
                for o, row in ((0, qrow), (1, krow)):
                    dve.wait_ge(s_abp, n + 3 + o)
                    if m and o == 0:
                        dve.wait_ge(s_abrow, m)
                    src = ps[:, 4 + (n + 2 + o) % 4, :]
                    if m == PROMPT:
                        ins = nc.vector.tensor_copy(row, src)
                    else:
                        v = "p (h d) -> p h d"
                        ins = rope(row.rearrange(v, d=64), src.rearrange(v, d=64), m, 64, 8)
                    link(ins)
                    dve.sem_inc(s_abd, 1)
                dve.wait_ge(s_aba, 3 * m + 2)
                if m == PROMPT:
                    tt(cvrow[:, 0:CKV], cvrow[:, 0:CKV], ckv_g[:], ALU.mult).then_inc(s_abrow, 1)
                else:
                    link(tt(cvrow[:, 0:CKV], cvrow[:, 0:CKV], ckv_g[:], ALU.mult))
                    kr = cvrow[:, CKV:].unsqueeze(1)
                    rope(kr, kr, m, 32, 1).then_inc(s_abrow, 1)
            ab_transposed(MT - 1)
            latents_transposed(CACHE_KT, 4 * MT + 2)

            def qb_transposed(m):
                dve.wait_ge(s_qbt, 2 * m + 1)
                nc.vector.tensor_copy(qbT[0:MQ, 0:4, m * P:(m + 1) * P],
                                      ps[0:MQ, (m % 2) * 2, :].rearrange("p (c t) -> p c t", c=4)).then_inc(s_qbtd, 1)

            for m in range(MT):
                dve.wait_ge(s_qba, 2 * m + 2)
                if m < PROMPT:
                    if m:
                        dve.wait_ge(s_qbr, m)
                    v = qbrow[m % 2].rearrange("p (h d) -> p h d", h=MH)[:, :, NOPE:]
                    rope(v, v, m, 32, MH).then_inc(s_qbr, 1)
                else:
                    dve.wait_ge(s_qbr, m)
                    dve.sem_inc(s_qbr, 1)
                if m:
                    qb_transposed(m - 1)
            qb_transposed(MT - 1)
            for i in range(8):
                n = 2 * i + 1 if i < 6 else 6 + i
                p, piece = divmod(i, 2)
                cols = slice(0, 512) if piece == 0 else slice(512, NKEY)
                w = 512 if piece == 0 else NKEY - 512
                dve.wait_ge(s_kvp, n + 1)
                nc.vector.tensor_copy(kbT[0:64, 2 * p, cols], ps[0:64, 4 + n % 4, 0:w])
                nc.vector.tensor_copy(kbT[0:64, 2 * p + 1, cols], ps[64:128, 4 + n % 4, 0:w]).then_inc(s_kvd, 1)

            def attention(l):
                U = units[l]
                n = len(U)
                for i in range(n + 3):
                    if i < n:
                        kind, m, h, kts = U[i]
                        w = len(kts) * P
                        dve.wait_ge(s_s.sem, s_s.at(l, i + 1))
                        sc = ps[:, 2 * (i % 2):2 * (i % 2) + 2, :].rearrange("p a b -> p (a b)")
                        if kind == "swa":
                            todo = []
                            if m != PROMPT:
                                for j, kt in enumerate(kts[:-1]):
                                    if kt != m:
                                        s = sc[:, j * P:(j + 1) * P]
                                        todo.append(tt(s, s, masks[kt - m], ALU.add))
                            todo.append(nc.vector.tensor_copy(sc[:, w:w + 1], sink8[:, h:h + 1]))
                            link(*todo)
                            w += 1
                        link(nc.vector.tensor_reduce(mxs[:, i % 4:i % 4 + 1], sc[:, 0:w], AX_X, ALU.max))
                        ts(nmx[:, i % 4:i % 4 + 1], mxs[:, i % 4:i % 4 + 1], -scale_of[kind], None, ALU.mult)\
                            .then_inc(s_nm.sem, 1)
                    if 1 <= i <= n and len(U[i - 1][3]) == 5:
                        dve.wait_ge(s_t.sem, s_t.at(l, i))
                        nc.vector.tensor_copy(pT[(i - 1) % 2][:, 4, :], ps[:, 5, 0:P]).then_inc(s_td.sem, 1)
                    if 2 <= i <= n + 1:
                        u = i - 2
                        kind, m, h, _ = U[u]
                        j = u // 2
                        col = slice(u % 4, u % 4 + 1)
                        dve.wait_ge(s_o.sem, s_o.at(l, u + 1))
                        link(nc.vector.reciprocal(rrec[:, col], rsum[:, col]))
                        if u % 2 == 0 and j >= 2:
                            dve.wait_ge(s_x.sem, s_x.at(l, j - 1))
                        if kind == "diff" and u % 2 == 0:
                            ts(o0[:], ps[:, 6, 0:P], rrec[:, col], None, ALU.mult).then_inc(s_oe.sem, 1)
                        elif kind == "diff":
                            link(ts(rrec[:, col], rrec[:, col], lam[:, 4:5], None, ALU.mult))
                            nc.vector.scalar_tensor_tensor(out=orow[:, j % 2, :], in0=ps[:, 6, 0:P], scalar=rrec[:, col],
                                                           in1=o0[:], op0=ALU.mult, op1=ALU.add).then_inc(s_oe.sem, 1)
                            dve.wait_ge(s_oe.sem, s_oe.at(l, u + 1))
                            link(nc.vector.tensor_tensor_reduce(out=osq[:], in0=orow[:, j % 2, :], in1=orow[:, j % 2, :],
                                                                scale=1.0, scalar=0.0, op0=ALU.mult, op1=ALU.add,
                                                                accum_out=ss[:, 12 + j % 2:13 + j % 2]))
                            variance(12 + j % 2, 1, P, out=s_ovar.sem)
                        else:
                            half = slice((u % 2) * 64, (u % 2) * 64 + 64)
                            ts(orow[:, j % 2, half], ps[:, 6, 0:64], rrec[:, col], None, ALU.mult).then_inc(s_oe.sem, 1)
                            if u % 2:
                                dve.wait_ge(s_oe.sem, s_oe.at(l, u + 1))
                                if l or j:
                                    dve.wait_ge(s_or.sem, s_or.at(l, j))
                                dve.sem_inc(s_or.sem, 1)
                    if i >= 4 and i % 2 == 0 and U[i - 4][0] == "diff":
                        j = (i - 4) // 2
                        dve.wait_ge(s_orstd.sem, s_orstd.at(l, j + 1))
                        ts(orow[:, j % 2, :], orow[:, j % 2, :], rstd[:, 12 + j % 2:13 + j % 2], None, ALU.mult)\
                            .then_inc(s_or.sem, 1)

            def out_and_norm2(l):
                dve.wait_ge(ld_gate.sem, ld_gate.at(l, 32))
                if l == 0:
                    dve.wait_ge(ld_x2, 32)
                dve.wait_ge(ld_bc.sem, ld_bc.at(l, 64))
                for m in range(MT + 2):
                    if m < MT:
                        for half in range(2):
                            j = 2 * m + half
                            cols = slice(half * 512, half * 512 + 512)
                            dve.wait_ge(s_op.sem, s_op.at(l, j + 1))
                            t = (prow_a, prow_b)[half]
                            tt(t, ps[:, j % 4, :], gate[cond(m)][:, cols], ALU.mult).then_inc(s_oped.sem, 1)
                            dve.wait_ge(s_oped.sem, s_oped.at(l, j + 1))
                            ins = tt(x_rows[:, m, cols], x_rows[:, m, cols], t, ALU.add)
                        ins.then_inc(s_xup.sem, 1)
                    if 1 <= m <= MT:
                        u = m - 1
                        dve.wait_ge(s_n2ss.sem, s_n2ss.at(l, u + 1))
                        variance(u, 1, D, out=s_n2var.sem)
                        if u >= 2:
                            dve.wait_ge(s_h2st[u % 2].sem, s_h2st[u % 2].at(l, 16 * (u // 2)))
                            dve.wait_ge(s_n2t.sem, s_n2t.at(l, u - 1))
                        dve.wait_ge(s_n2r.sem, s_n2r.at(l, u + 1))
                        h2 = xg[l][u % 2]
                        link(nc.vector.scalar_tensor_tensor(out=h2, in0=x_rows[:, u, :], scalar=rstd[:, u:u + 1],
                                                            in1=bc[l][:, cond(u), :], op0=ALU.mult, op1=ALU.mult))
                        tt(h2, h2, bc[l][:, 2 + cond(u), :], ALU.add).then_inc(s_h2.sem, 1)
                    if m >= 2:
                        u = m - 2
                        dve.wait_ge(s_n2t.sem, s_n2t.at(l, u + 1))
                        nc.vector.tensor_copy(xgT[l][u % 2][:, 4:8, :], ps[:, 5, :].rearrange("p (c t) -> p c t", c=4))\
                            .then_inc(s_n2d.sem, 1)

            def first_of(v, out):
                m4 = mx5.unsqueeze(2).broadcast_to([P, MT, 4])
                code = cst[:, C_CODE:C_CODE + 4].unsqueeze(1).broadcast_to([P, MT, 4])
                link(nc.vector.tensor_reduce(mx5, v, AX_X, ALU.max))
                link(tt(eqt, v, m4, ALU.is_equal))
                link(tt(eqt, eqt, code, ALU.mult))
                link(nc.vector.tensor_reduce(mx5, eqt, AX_X, ALU.max))
                link(tt(out, eqt, m4, ALU.is_equal))

            def route(l):
                sc4 = scores[:].rearrange("p m (g e) -> p m g e", g=NG)
                dve.wait_ge(s_rx.sem, s_rx.at(l, MT))
                link(ts(scores[:], scores[:], 1.0, None, ALU.add))
                link(nc.vector.reciprocal(scores[:], scores[:]))
                link(tt(sel.rearrange("p m g e -> p m (g e)"), scores[:], rbias[:].unsqueeze(1).broadcast_to([P, MT, E]), ALU.add))
                s20 = sel.rearrange("p m g e -> p (m g) e")
                link(tt(pairs[:, :, 0:3], s20[:, :, 0:3], s20[:, :, 1:4], ALU.add),
                     tt(pairs[:, :, 3:5], s20[:, :, 0:2], s20[:, :, 2:4], ALU.add),
                     tt(pairs[:, :, 5:6], s20[:, :, 0:1], s20[:, :, 3:4], ALU.add))
                link(nc.vector.tensor_reduce(gs.rearrange("p m g -> p (m g)"), pairs, AX_X, ALU.max))
                first_of(gs, goh)
                link(tt(prod, sel, goh.unsqueeze(3).broadcast_to([P, MT, NG, EPG]), ALU.mult))
                link(nc.vector.tensor_reduce(ing, prod.rearrange("p m g e -> p m e g"), AX_X, ALU.add))
                first_of(ing, oh1)
                link(nc.vector.scalar_tensor_tensor(out=ing2, in0=oh1, scalar=NEG, in1=ing, op0=ALU.mult, op1=ALU.add))
                first_of(ing2, oh2)
                for o, oh in ((o1, oh1), (o2, oh2)):
                    link(tt(o, goh.unsqueeze(3).broadcast_to([P, MT, NG, EPG]),
                            oh.unsqueeze(2).broadcast_to([P, MT, NG, EPG]), ALU.mult))
                tt(mask, o1, o2, ALU.add).then_inc(s_mask.sem, 1)
                for w, o in ((0, o1), (1, o2)):
                    link(tt(prod, sc4, o, ALU.mult))
                    link(nc.vector.tensor_reduce(wsel[:, w, :], prod.rearrange("p m g e -> p m (g e)"), AX_X, ALU.add))
                link(tt(wsel[:, 2, :], wsel[:, 0, :], wsel[:, 1, :], ALU.add))
                link(nc.vector.reciprocal(wsel[:, 3, :], wsel[:, 2, :]))
                for w in range(2):
                    link(tt(wsel[:, w, :], wsel[:, w, :], wsel[:, 3, :], ALU.mult))
                dve.wait_ge(s_cnt.sem, s_cnt.at(l, 1))
                v = "p (m e) -> p m e"
                link(nc.vector.tensor_copy(cum, ps[:, 7, 0:80].rearrange(v, e=E)),
                     nc.vector.tensor_copy(tot, ps[:, 7, 80:160].rearrange(v, e=E)),
                     nc.vector.memset(pref[:, 0, :], 0.0))
                for m in range(1, MT):
                    link(tt(pref[:, m, :], pref[:, m - 1, :], tot[:, m - 1, :], ALU.add))
                link(tt(cnt, pref[:, MT - 1, :], tot[:, MT - 1, :], ALU.add))
                link(tt(cum, cum, pref, ALU.add))
                link(tt(thr_hit, cnt.unsqueeze(2).broadcast_to([P, E, MT]),
                        cst[:, C_THR:C_THR + 80].rearrange("p (e k) -> p e k", e=E), ALU.is_gt))
                link(nc.vector.tensor_reduce(ntile, thr_hit, AX_X, ALU.add))
                link(tt(le_hit, ntile.unsqueeze(1).broadcast_to([P, E, E]),
                        cst[:, C_LE:C_LE + E * E].rearrange("p (e k) -> p e k", e=E), ALU.mult))
                link(nc.vector.tensor_reduce(ends, le_hit, AX_X, ALU.add))
                link(tt(starts, ends, ntile, ALU.subtract))
                link(ts(starts, starts, float(P), None, ALU.mult))
                link(tt(slot, cum, starts.unsqueeze(1).broadcast_to([P, MT, E]), ALU.add))
                for w, o in ((0, o1), (1, o2)):
                    link(tt(prod.rearrange("p m g e -> p m (g e)"), slot, o.rearrange("p m g e -> p m (g e)"), ALU.mult))
                    link(nc.vector.tensor_reduce(mx5, prod.rearrange("p m g e -> p m (g e)"), AX_X, ALU.add))
                    link(nc.vector.tensor_copy(slots[:, w, :], mx5))
                hit = yr[0][:, 0:NT * E].rearrange("p (t e) -> p t e", e=E)
                link(tt(hit, ends.unsqueeze(1).broadcast_to([P, NT, E]),
                        cst[:, C_IOTA:C_IOTA + NT * E].rearrange("p (t e) -> p t e", e=E), ALU.is_le))
                link(nc.vector.tensor_reduce(eidf[:], hit, AX_X, ALU.add))
                link(ts(eidf[:], eidf[:], float(E - 1), None, ALU.min))
                nc.vector.tensor_copy(eidi[:], eidf[:]).then_inc(s_slots.sem, 1)
                dve.wait_ge(s_idt.sem, s_idt.at(l, 1))
                nc.vector.tensor_copy(idall[:], ps[:, 3, 0:NT]).then_inc(s_ids.sem, 1)

            def experts(l):
                def gathered(i, b):
                    t = 2 * i + b
                    dve.wait_ge(s_mt[l], t + 1)
                    nc.vector.tensor_copy(xgT[l][b][:, 4:8, :], ps[:, 1, :].rearrange("p (c t) -> p c t", c=4))\
                        .then_inc(s_xed[l], 1)
                    dve.wait_ge(s_ex[l], t + 1)
                    ts(ebuf[b], ebuf[b], 1.0, None, ALU.add).then_inc(s_mc[l], 1)
                    dve.wait_ge(s_mc[l], 3 * t + 1)
                    nc.vector.reciprocal(ebuf[b], ebuf[b]).then_inc(s_mc[l], 1)
                    dve.wait_ge(s_mc[l], 3 * t + 2)
                    tt(ebuf[b], ps[:, 2 + b, 0:2 * P], ebuf[b], ALU.mult).then_inc(s_mc[l], 1)
                    dve.wait_ge(s_mc[l], 3 * t + 3)
                    tt(aT[b], ps[:, 2 + b, 2 * P:4 * P], ebuf[b], ALU.mult).then_inc(s_act[l], 1)

                def out_rows(i, b):
                    dve.wait_ge(s_dn[l], 2 * i + b + 1)
                    dve.wait_ge(s_yw[l][b], 16 * i + 16)
                    nc.vector.tensor_copy(yr[b][:, 512:D], ps[:, 5 + 2 * b, :]).then_inc(s_yed[l], 1)

                dve.sem_inc(s_yed[l], 2)
                gathered(0, 0)
                with dve.Fori(0, NP) as i:
                    gathered(i, 1)
                    out_rows(i, 0)
                    gathered(i + 1, 0)
                    out_rows(i, 1)
                out_rows(NP, 0)

            def combine(l):
                dve.wait_ge(ld_gate2.sem, ld_gate2.at(l, 32))
                for m in range(MT):
                    a, b = yc[2 * m], yc[2 * m + 1]
                    dve.wait_ge(s_yc[m].sem, s_yc[m].at(l, 32))
                    link(ts(a, a, wsel[:, 0, m:m + 1], None, ALU.mult))
                    link(nc.vector.scalar_tensor_tensor(out=a, in0=b, scalar=wsel[:, 1, m:m + 1], in1=a,
                                                        op0=ALU.mult, op1=ALU.add))
                    link(tt(a, a, gate[cond(m)], ALU.mult))
                    tt(x_rows[:, m, :], x_rows[:, m, :], a, ALU.add).then_inc(s_comb[l], 1)

            prow_a, prow_b = view(ST, 8 * KB, 512), view(ST, 10 * KB, 512)
            dve.wait_ge(s_about, 64)
            attention(0)
            out_and_norm2(0)
            route(0)
            ada(1)
            experts(0)
            combine(0)

            dve.wait_ge(s_ss.sem, s_ss.at(1, MT))
            variance(0, MT, D, out=s_var.sem)
            dve.wait_ge(s_rstd.sem, s_rstd.at(1, 1))
            norm1(1)

            dve.wait_ge(s_adast, 32)

            def sw_transposed(m):
                dve.wait_ge(s_swt, 3 * m + 2)
                nc.vector.tensor_copy(qsT[:, 4:8, m * P:(m + 1) * P], ps[:, 1, :].rearrange("p (c t) -> p c t", c=4))\
                    .then_inc(s_swtd, 1)

            v = "p (h d) -> p h d"
            for m in range(MT):
                for o in range(3):
                    n = 3 * m + o
                    dve.wait_ge(s_swp, n + 1)
                    if n:
                        dve.wait_ge(s_swd, n)
                    if o == 0 and m:
                        sw_transposed(m - 1)
                        dve.wait_ge(s_swt, 3 * m)
                    src = ps[:, 4 + n % 4, :]
                    if o < 2:
                        row = qsrow[:, o * 512:(o + 1) * 512]
                        if m == PROMPT:
                            ins = nc.vector.tensor_copy(row, src)
                        else:
                            ins = rope(row.rearrange(v, d=64), src.rearrange(v, d=64), m, 64, 8)
                        ins.then_inc(s_swd, 1)
                        continue
                    kt = PROMPT_KT if m == PROMPT else m
                    ks = src[:, 0:256].rearrange(v, d=64)
                    if m == PROMPT:
                        link(nc.vector.tensor_copy(ksrow[:, :, 0, :], ks))
                    else:
                        link(rope(ksrow[:, :, 0, :], ks, m, 64, 4))
                    link(nc.vector.tensor_copy(vs[:, kt, :], src[:, 256:512]),
                         nc.vector.tensor_copy(ksrow[:, :, 1, :], ksrow[:, :, 0, :]))
                    dve.sem_inc(s_swd, 1)
                    dve.sem_inc(s_swrow, 1)
            sw_transposed(MT - 1)
            dve.wait_ge(s_swout, 32)
            attention(1)
            out_and_norm2(1)
            route(1)
            experts(1)
            combine(1)
            dve.wait_ge(ld_fg, 16)
            for m in range(MT):
                dve.wait_ge(s_fss, m + 1)
                variance(m, 1, D, out=s_fvar)
            for m in range(MT):
                dve.wait_ge(s_fr, m + 1)
                nc.vector.scalar_tensor_tensor(out=x_rows[:, m, :], in0=x_rows[:, m, :], scalar=rstd[:, m:m + 1],
                                               in1=bc[1][:, 0, :], op0=ALU.mult, op1=ALU.mult).then_inc(s_fy, 1)

        @block.tensor
        def _(pe):
            mm = nc.tensor.matmul
            pe.wait_ge(s_csil, 1)
            pe.wait_ge(ld_cst, 16)

            def ada(l, first, end):
                for n in range(first, end):
                    i = 12 * l + n
                    if n < 12:
                        pe.wait_ge(ld_ada[i % 3], 16 * (i // 3 + 1))
                        if i >= 2:
                            pe.wait_ge(s_adaev, i - 1)
                        for k in range(KC):
                            ins = mm(ps[0:2, 4 + i % 2, :], csil[:, :, k], ada_ring[l][i % 3][:, k, :],
                                     start=(k == 0), stop=(k == KC - 1))
                        ins.then_inc(s_adamm, 1)
                    if n:
                        pe.wait_ge(s_adaev, i)
                        for j in range(4):
                            at = 4 * (n - 1) + j
                            ins = nc.tensor.transpose(ps[:, l, at:at + 49:48],
                                                      ada_out[l][(i - 1) % 2][0:2, j * P:(j + 1) * P], ident[0:2, 0:2])
                        ins.then_inc(s_adatr, 1)

            def ada_finish(l):
                pe.wait_ge(s_adac, l + 1)
                nc.tensor.transpose(ps[0:96, 2 + l, 0:P], acol[l], ident).then_inc(s_adat, 1)
                pe.wait_ge(s_adar, l + 1)
                nc.tensor.transpose(ps[:, 4 + l, 0:96], arow[l][0:96, :], ident[0:96, 0:96]).then_inc(s_adat2, 1)
                pe.wait_ge(s_adacol, l + 1)

            def norm1(l):
                for m in range(MT):
                    pe.wait_ge(s_xn.sem, s_xn.at(l, m + 1))
                    if m >= 2:
                        pe.wait_ge(s_n1a.sem, s_n1a.at(l, m - 1))
                        pe.wait_ge(s_n1d.sem, s_n1d.at(l, m - 1))
                    for k in range(KC):
                        ins = nc.tensor.transpose(ps[:, (m % 2) * 2 + k // 4, (k % 4) * P:(k % 4 + 1) * P],
                                                  xn[m % 2][:, k * P:(k + 1) * P], ident)
                    ins.then_inc(s_n1t.sem, 1)
                pe.wait_ge(s_n1a.sem, s_n1a.at(l, MT))
                pe.wait_ge(s_n1d.sem, s_n1d.at(l, MT))

            ada(0, 0, 13)
            ada_finish(0)
            norm1(0)
            pe.wait_ge(ld_win, 64)

            def ab_bank_free(n):
                if n < 4:
                    return
                m, o = divmod(n - 4, 5)
                if o in (2, 3):
                    pe.wait_ge(s_abd, 2 * m + o - 1)
                else:
                    pe.wait_ge(s_aba, 3 * m + min(o, 2) + 1)

            def ab_transposes(m, q, k, ql, cv):
                if m:
                    pe.wait_ge(s_abta, 2 * m)
                    pe.wait_ge(s_abtd, 2 * m)
                for bank, row, n in ((0, q, 4), (1, k, 4), (2, ql, 3)):
                    if row is None:
                        continue
                    for c in range(n):
                        ins = nc.tensor.transpose(ps[:, bank, c * P:(c + 1) * P], row[:, c * P:(c + 1) * P], ident)
                    ins.then_inc(s_abt, 1)
                for c in range(2):
                    nc.tensor.transpose(ps[:, 3, c * P:(c + 1) * P], cv[:, c * P:(c + 1) * P], ident)
                nc.tensor.transpose(ps[0:KR, 3, 2 * P:3 * P], cv[:, CKV:CKV + KR], ident).then_inc(s_abt, 1)

            def ab_rows_ready(m):
                pe.wait_ge(s_abd, 2 * m + 2)
                pe.wait_ge(s_abrow, m + 1)

            for m in range(MT):
                for o, grp in enumerate(AB_ORDER):
                    n = 5 * m + o
                    at, w = AB_COLS[grp]
                    ab_bank_free(n)
                    for k in range(KC):
                        ins = mm(ps[:, 4 + n % 4, 0:w], hT[:, k, m * P:(m + 1) * P], w_in[:, k, at:at + w],
                                 start=(k == 0), stop=(k == KC - 1))
                    ins.then_inc(s_abp, 1)
                    if o == 1 and m:
                        ab_rows_ready(m - 1)
                        ab_transposes(m - 1, qrow, krow, qlrow, cvrow)
            ab_rows_ready(MT - 1)
            ab_transposes(MT - 1, qrow, krow, qlrow, cvrow)
            pe.wait_ge(ld_cache, 48)
            ab_transposes(MT, None, cache_k, None, cache_c)

            pe.wait_ge(ld_lat, 80)
            pe.wait_ge(s_aba, 3 * MT)
            pe.wait_ge(s_abta, 2 * MT + 1)
            pe.wait_ge(s_abtd, 2 * MT + 1)

            def qb_transposes(m):
                pe.wait_ge(s_qbr, m + 1)
                if m >= 2:
                    pe.wait_ge(s_qbta, m - 1)
                    pe.wait_ge(s_qbtd, m - 1)
                for h in range(MH):
                    ins = nc.tensor.transpose(ps[0:MQ, (m % 2) * 2 + h // 4, (h % 4) * P:(h % 4 + 1) * P],
                                              qbrow[m % 2][:, h * MQ:(h + 1) * MQ], ident)
                    if h % 4 == 3:
                        ins.then_inc(s_qbt, 1)

            for m in range(MT + 1):
                if m < MT:
                    for half in range(2):
                        j = 2 * m + half
                        if j >= 4:
                            pe.wait_ge(s_qba, j - 3)
                        for k in range(3):
                            ins = mm(ps[:, 4 + j % 4, 0:384], qlT[:, k, m * P:(m + 1) * P],
                                     wqb[:, k, half * 384:(half + 1) * 384], start=(k == 0), stop=(k == 2))
                        ins.then_inc(s_qbp, 1)
                if m:
                    qb_transposes(m - 1)
            pe.wait_ge(s_qba, 2 * MT)
            for n in range(14):
                is_v = n < 12 and n % 2 == 0
                if n >= 4:
                    b = n - 4
                    if b < 12 and b % 2 == 0:
                        pe.wait_ge(s_kva, b // 2 + 1)
                    else:
                        pe.wait_ge(s_kvd, b // 2 + 1)
                for k in range(2):
                    if is_v:
                        kt = n // 2
                        ins = mm(ps[:, 4 + n % 4, :], ckvT[:, k, kt * P:(kt + 1) * P], wkvb[:, k, 512:1024],
                                 start=(k == 0), stop=(k == 1))
                    else:
                        p, piece = divmod(n // 2 if n < 12 else n - 6, 2)
                        cols = slice(0, 512) if piece == 0 else slice(512, NKEY)
                        w = 512 if piece == 0 else NKEY - 512
                        ins = mm(ps[:, 4 + n % 4, 0:w], wkvb[:, k, p * P:(p + 1) * P], ckvT[:, k, cols],
                                 start=(k == 0), stop=(k == 1))
                ins.then_inc(s_kvp, 1)
            pe.wait_ge(s_kva, 6)
            pe.wait_ge(s_kvd, 8)
            pe.wait_ge(s_krc, 8)
            pe.wait_ge(s_qbta, MT)
            pe.wait_ge(s_qbtd, MT)
            pe.wait_ge(ld_vcache, 16)
            pe.wait_ge(s_about, 64)

            def attention(l):
                U = units[l]
                n = len(U)
                for i in range(n + 5):
                    if i < n:
                        u = U[i]
                        if i >= 2:
                            pe.wait_ge(s_p.sem, s_p.at(l, i - 1))
                        for col, kt, w in pieces(u[3]):
                            ins = mm(ps[:, 2 * (i % 2) + col // 512, col % 512:col % 512 + w * P], q_of(l, u),
                                     k_of(l, u, kt, w), start=True, stop=True)
                        ins.then_inc(s_s.sem, 1)
                    if 1 <= i <= n:
                        u = i - 1
                        pe.wait_ge(s_p.sem, s_p.at(l, u + 1))
                        if u:
                            pe.wait_ge(s_ta.sem, s_ta.at(l, u))
                            if wide(l, u):
                                pe.wait_ge(s_td.sem, s_td.at(l, wide(l, u)))
                        for j in range(len(U[u][3])):
                            ins = nc.tensor.transpose(ps[:, 4 + j // 4, (j % 4) * P:(j % 4 + 1) * P],
                                                      prow[u % 2][:, j * P:(j + 1) * P], ident)
                        ins.then_inc(s_t.sem, 1)
                    if 2 <= i <= n + 1:
                        u = i - 2
                        pe.wait_ge(s_ta.sem, s_ta.at(l, u + 1))
                        if wide(l, u + 1):
                            pe.wait_ge(s_td.sem, s_td.at(l, wide(l, u + 1)))
                        if u:
                            pe.wait_ge(s_oe.sem, s_oe.at(l, u))
                        kts = U[u][3]
                        for j, kt in enumerate(kts):
                            ins = mm(ps[:, 6, 0:v_width(U[u])], pT[u % 2][:, j, :], v_of(l, U[u], kt),
                                     start=(j == 0), stop=(j == len(kts) - 1))
                        ins.then_inc(s_o.sem, 1)
                    if i >= 5 and i % 2:
                        j = (i - 5) // 2
                        pe.wait_ge(s_or.sem, s_or.at(l, j + 1))
                        if j:
                            pe.wait_ge(s_xe.sem, s_xe.at(l, j))
                        nc.tensor.transpose(ps[:, 7, 0:P], orow[:, j % 2, :], ident).then_inc(s_x.sem, 1)

            def out_and_router(l, w_out):
                pe.wait_ge(s_xe.sem, s_xe.at(l, len(units[l]) // 2))
                pe.wait_ge(ld_wout.sem, ld_wout.at(l, 16))
                for m in range(MT + 3):
                    if m < MT:
                        for half in range(2):
                            j = 2 * m + half
                            if j >= 4:
                                pe.wait_ge(s_oped.sem, s_oped.at(l, j - 3))
                            for k in range(KC):
                                ins = mm(ps[:, j % 4, :], hT[:, k, m * P:(m + 1) * P],
                                         w_out[:, k, half * 512:(half + 1) * 512], start=(k == 0), stop=(k == KC - 1))
                            ins.then_inc(s_op.sem, 1)
                    if 2 <= m <= MT + 1:
                        u = m - 2
                        pe.wait_ge(s_h2.sem, s_h2.at(l, u + 1))
                        if u:
                            pe.wait_ge(s_n2a.sem, s_n2a.at(l, u))
                            pe.wait_ge(s_n2d.sem, s_n2d.at(l, u))
                        for k in range(KC):
                            ins = nc.tensor.transpose(ps[:, 4 + k // 4, (k % 4) * P:(k % 4 + 1) * P],
                                                      xg[l][u % 2][:, k * P:(k + 1) * P], ident)
                        ins.then_inc(s_n2t.sem, 1)
                    if m >= 3:
                        u = m - 3
                        pe.wait_ge(s_n2a.sem, s_n2a.at(l, u + 1))
                        pe.wait_ge(s_n2d.sem, s_n2d.at(l, u + 1))
                        if u:
                            pe.wait_ge(s_rx.sem, s_rx.at(l, u))
                        for k in range(KC):
                            ins = mm(ps[:, 6, 0:E], xgT[l][u % 2][:, k, :], rw[:, k, :], start=(k == 0), stop=(k == KC - 1))
                        ins.then_inc(s_rt.sem, 1)
                pe.wait_ge(s_mask.sem, s_mask.at(l, 1))
                m80 = mask.rearrange("p m g e -> p (m g e)")
                mm(ps[:, 7, 0:80], tri, m80, start=True, stop=True)
                mm(ps[:, 7, 80:160], ones, m80, start=True, stop=True).then_inc(s_cnt.sem, 1)
                if l == 0:
                    ada(1, 0, 5)
                pe.wait_ge(s_idl.sem, s_idl.at(l, 16))
                nc.tensor.transpose(ps[:, 3, 0:NT], idrow[0:NT, :], ident[0:NT, 0:NT]).then_inc(s_idt.sem, 1)
                if l == 0:
                    ada(1, 5, 13)
                pe.wait_ge(s_ids.sem, s_ids.at(l, 1))
                if l == 0:
                    ada_finish(1)

            def experts(l):
                def gathered(i, b):
                    t = 2 * i + b
                    pe.wait_ge(s_xg[l][b], 16 * i + 16)
                    if not (isinstance(t, int) and t == 0):
                        pe.wait_ge(s_xea[l], t)
                        pe.wait_ge(s_xed[l], t)
                    for k in range(KC):
                        ins = nc.tensor.transpose(ps[:, k // 4, (k % 4) * P:(k % 4 + 1) * P],
                                                  xg[l][b][:, k * P:(k + 1) * P], ident)
                    ins.then_inc(s_mt[l], 1)
                    pe.wait_ge(s_wgu[l][b], 32 * i + 32)
                    pe.wait_ge(s_xea[l], t + 1)
                    pe.wait_ge(s_xed[l], t + 1)
                    for q, w in enumerate((wg[b], wg[b], wu[b], wu[b])):
                        for k in range(KC):
                            ins = mm(ps[:, 2 + b, q * P:(q + 1) * P], w[:, k, (q % 2) * P:(q % 2 + 1) * P],
                                     xgT[l][b][:, k, :], start=(k == 0), stop=(k == KC - 1))
                    ins.then_inc(s_gu[l], 1)

                def down(i, b):
                    t = 2 * i + b
                    pe.wait_ge(s_wd[l][b], 16 * i + 16)
                    pe.wait_ge(s_act[l], t + 1)
                    pe.wait_ge(s_yea[l], t + 1)
                    pe.wait_ge(s_yed[l], t + 1)
                    for half in range(2):
                        for q in range(2):
                            ins = mm(ps[:, 4 + 2 * b + half, :], aT[b][:, q * P:(q + 1) * P],
                                     wd[b][:, q, half * 512:(half + 1) * 512], start=(q == 0), stop=(q == 1))
                    ins.then_inc(s_dn[l], 1)

                gathered(0, 0)
                with pe.Fori(0, NP) as i:
                    gathered(i, 1)
                    down(i, 0)
                    gathered(i + 1, 0)
                    down(i, 1)
                down(NP, 0)

            attention(0)
            out_and_router(0, w_abo)
            experts(0)
            norm1(1)

            def sw_transposes(m, q, k):
                if m:
                    pe.wait_ge(s_swta, 2 * m)
                    pe.wait_ge(s_swtd, m)
                if q is not None:
                    for c in range(KC):
                        ins = nc.tensor.transpose(ps[:, c // 4, (c % 4) * P:(c % 4 + 1) * P], q[:, c * P:(c + 1) * P], ident)
                        if c % 4 == 3:
                            ins.then_inc(s_swt, 1)
                for c in range(4):
                    ins = nc.tensor.transpose(ps[:, 2, c * P:(c + 1) * P], k[:, c * P:(c + 1) * P], ident)
                ins.then_inc(s_swt, 1)

            krows = ksrow.rearrange("p h t d -> p (h t d)")
            pe.wait_ge(ld_wswa, 16)
            for m in range(MT):
                for o in range(3):
                    n = 3 * m + o
                    if n >= 4:
                        pe.wait_ge(s_swd, n - 3)
                    for k in range(KC):
                        ins = mm(ps[:, 4 + n % 4, :], hT[:, k, m * P:(m + 1) * P], w_swa[:, k, o * 512:(o + 1) * 512],
                                 start=(k == 0), stop=(k == KC - 1))
                    ins.then_inc(s_swp, 1)
                    if o == 0 and m:
                        pe.wait_ge(s_swd, 3 * m)
                        sw_transposes(m - 1, qsrow, krows)
            pe.wait_ge(s_swd, 3 * MT)
            sw_transposes(MT - 1, qsrow, krows)
            pe.wait_ge(ld_scache, 48)
            sw_transposes(MT, None, cache_k)
            pe.wait_ge(s_swta, 2 * MT + 1)
            pe.wait_ge(s_swtd, MT)
            attention(1)
            out_and_router(1, w_swao)
            experts(1)


_INS = ['x_prompt', 'x_sample', 'cache_diff_k', 'cache_diff_v', 'cache_mla_ckv', 'cache_mla_krope', 'cache_swa_k',
        'cache_swa_v', 'c', 'c_ctx', 'ada_w', 'ada_b', 'norm1_g', 'norm2_g', 'final_norm_g', 'ab_w_in', 'diff_lambda',
        'diff_subln_g', 'mla_q_norm_g', 'mla_w_qb', 'mla_kv_norm_g', 'mla_w_kvb', 'ab_w_out', 'swa_w_in', 'swa_sink',
        'swa_w_out', 'router_w', 'router_bias', 'moe_w_gate', 'moe_w_up', 'moe_w_down']
_OUTS = [((1, 128, 1024), 'float32'), ((1, 512, 1024), 'float32'), ((1, 1, 128, 4, 2, 64), 'float32'),
         ((1, 1, 128, 4, 128), 'float32'), ((1, 1, 128, 256), 'float32'), ((1, 1, 128, 32), 'float32'),
         ((1, 1, 128, 4, 64), 'float32'), ((1, 1, 128, 4, 64), 'float32')]


def kernel(**inputs):
    import numpy as _np
    import concourse.bacc as _bacc
    from concourse import mybir as _mybir
    from concourse.bass_utils import run_bass_kernel_spmd as _run

    nc = _bacc.Bacc("TRN2", target_bir_lowering=False, num_devices=1)
    arrays, args = {}, []
    for name in _INS + ['consts']:
        a = constants() if name == 'consts' else _np.ascontiguousarray(inputs[name])
        arrays[f"in_{name}_dram"] = a
        args.append(nc.dram_tensor(f"in_{name}_dram", a.shape, _mybir.dt.from_np(a.dtype), kind="ExternalInput").ap())
    for i, (shape, dtype) in enumerate(_OUTS):
        dt = _mybir.dt.from_np(_np.dtype(dtype))
        args.append(nc.dram_tensor(f"out_{i}_dram", shape, dt, kind="ExternalOutput").ap())
    build(nc, *args)
    r = _run(nc, [arrays], core_ids=[0])
    return tuple(r.results[0][f"out_{i}_dram"] for i in range(len(_OUTS)))
```

```python
import math
from contextlib import ExitStack

import numpy as np

import concourse.bass as bass
from concourse import mybir

F32 = mybir.dt.float32
I32 = mybir.dt.int32
ALU = mybir.AluOpType
ACT = mybir.ActivationFunctionType
AX_X = mybir.AxisListType.X

P = 128
D = 1024
KC = D // P
MT = 5
PROMPT = 4
KT = 6
CACHE_KT, PROMPT_KT = 4, 5
NKEY = KT * P
AB_IN = 2208
QL, CKV, KR = 384, 256, 32
MH, NOPE, MQ = 8, 64, 96
E, F = 16, 256
NG, EPG = 4, 4
NT = (MT * P * 2 + E * (P - 1)) // P
EPS = 1e-6
NEG = -1e30
LAMBDA_INIT = 0.8 - 0.6 * math.exp(-0.3 * 0)
SWA_IN = 1536
KB = 256
SW = MT * P

(C_ID, C_TRI, C_ONE, C_M1, C_M2, C_C64, C_S64, C_C32, C_S32, C_THR, C_IOTA, C_LE, C_CODE, C_TOK, C_SCL,
 C_LO, NCONST) = np.cumsum([0, P, P, P, P, P, 256, 256, P, P, 80, NT * E, E * E, 4, MT, 1, P]).tolist()


def constants():
    c = np.zeros((P, NCONST), np.float32)
    i = np.arange(P)
    c[:, C_ID:C_ID + P] = np.eye(P)
    c[:, C_TRI:C_TRI + P] = i[:, None] < i[None, :]
    c[:, C_ONE:C_ONE + P] = 1.0
    c[:, C_M1:C_M1 + P] = np.where(i[None, :] >= i[:, None], 0.0, NEG)
    c[:, C_M2:C_M2 + P] = np.where(i[None, :] <= i[:, None], 0.0, NEG)
    pos = np.arange(4 * P)
    for dim, cc, cs in ((64, C_C64, C_S64), (32, C_C32, C_S32)):
        nf = dim // 4
        inv = np.float32(10000.0) ** (-np.arange(nf, dtype=np.float32) / np.float32(nf))
        ang = np.concatenate([(pos // 64).astype(np.float32)[:, None] * inv,
                              (pos % 64).astype(np.float32)[:, None] * inv], -1)
        co = np.repeat(np.cos(ang), 2, -1)
        si = np.repeat(np.sin(ang), 2, -1)
        si[:, 0::2] *= -1
        for m in range(4):
            c[:, cc + m * dim:cc + (m + 1) * dim] = co[m * P:(m + 1) * P]
            c[:, cs + m * dim:cs + (m + 1) * dim] = si[m * P:(m + 1) * P]
    c[:, C_THR:C_THR + 80] = np.tile(np.arange(MT) * P, E)
    c[:, C_IOTA:C_IOTA + NT * E] = np.repeat(np.arange(NT), E)
    c[:, C_LE:C_LE + E * E] = (np.arange(E)[None, :] <= np.arange(E)[:, None]).reshape(-1)
    c[:, C_CODE:C_CODE + 4] = 4 - np.arange(4)
    c[:, C_TOK:C_TOK + MT] = i[:, None] + P * np.arange(MT)[None, :]
    c[:, C_LO:C_LO + P] = np.arange(P) - P
    c[:96, C_SCL] = np.isin(np.arange(96) % 48 // 8, (1, 4))
    return c


def attention_units(l):
    heads = [("diff", h) for h in range(8)] + [("mla", h) for h in range(8)] if l == 0 else \
        [("swa", h) for h in range(16)]
    units = []
    for p in range(len(heads) // 2):
        for m in range(MT):
            for kind, h in heads[2 * p:2 * p + 2]:
                if m == PROMPT:
                    kts = [PROMPT_KT]
                elif kind == "swa":
                    kts = [t for t in (m - 1, m, m + 1) if 0 <= t < 4] + [CACHE_KT]
                else:
                    kts = [0, 1, 2, 3, CACHE_KT]
                units.append((kind, m, h, kts))
    return units


def pieces(kts):
    out = []
    for j, t in enumerate(kts):
        if out and t == out[-1][1] + out[-1][2] and j % 4:
            out[-1][2] += 1
        else:
            out.append([j * P, t, 1])
    return out


def build(nc, x_prompt, x_sample, cache_diff_k, cache_diff_v, cache_mla_ckv, cache_mla_krope, cache_swa_k,
          cache_swa_v, c_s, c_ctx, ada_w, ada_b, norm1_g, norm2_g, final_norm_g, ab_w_in, diff_lambda,
          diff_subln_g, mla_q_norm_g, mla_w_qb, mla_kv_norm_g, mla_w_kvb, ab_w_out, swa_w_in, swa_sink,
          swa_w_out, router_w, router_bias, moe_w_gate, moe_w_up, moe_w_down, consts,
          y_prompt, y_sample, new_diff_k, new_diff_v, new_mla_ckv, new_mla_krope, new_swa_k, new_swa_v):
    with ExitStack() as ctx:
        def sb(name, shape, dt=F32):
            return ctx.enter_context(nc.sbuf_tensor(name, shape, dt))

        def sem(name):
            return ctx.enter_context(nc.semaphore(name))

        def per_layer(name):
            return [sem(f"{name}_l{l}") for l in range(2)]

        def scratch(name, shape, dt=F32):
            return nc.dram_tensor(name, shape, dt, kind="Internal").ap()

        class Repeated:

            def __init__(self, name, total):
                self.sem, self.total = sem(name), total

            def at(self, l, n):
                return l * self.total + n

        ps = ctx.enter_context(nc.psum_tensor("ps", [P, 8, 512], F32))

        X = sb("x_rows", [P, MT * D])
        H = sb("region_h", [P, 20 * KB])
        A = sb("region_a", [P, 80 * KB])
        B = sb("region_b", [P, 48 * KB])
        ST = sb("region_st", [P, 25 * KB // 2])
        G = sb("region_g", [P, 8 * KB])
        cst = sb("cst", [P, NCONST])

        def view(region, at, *dims):
            v = region[:, at:at + int(np.prod(dims))]
            names = "abcd"[:len(dims)]
            if len(dims) > 1:
                v = v.rearrange(f"p ({' '.join(names)}) -> p {' '.join(names)}", **dict(zip(names[1:], dims[1:])))
            return v

        ident = cst[:, C_ID:C_ID + P]
        tri = cst[:, C_TRI:C_TRI + P]
        ones = cst[:, C_ONE:C_ONE + P]
        masks = {-1: cst[:, C_M1:C_M1 + P], 1: cst[:, C_M2:C_M2 + P]}

        x_rows = view(X, 0, MT, D)
        vd = view(X, 0, KT, 512)
        hT = view(H, 0, KC, MT * P)
        w_in = view(A, 0, KC, AB_IN)
        qaT = view(A, KC * AB_IN, 4, MT * P)
        qbT = view(A, 0, MH, MT * P)
        kbT = view(A, 20 * KB, MH, NKEY)
        vb = view(A, 44 * KB, KT, 512)
        w_swa = view(A, 0, KC, SWA_IN)
        w_swao = view(A, 48 * KB, KC, D)
        ada_ring = [[view(R, i * 16 * KB, KC, 512) for i in range(3)] for R in (B, A)]
        wqb = view(B, 0, 3, 768)
        wkvb = view(B, 9 * KB, 2, 1024)
        qlT = view(B, 17 * KB, 3, MT * P)
        krT = view(B, 17 * KB + 1920, NKEY)
        ckvT = view(B, 17 * KB + 1920 + 768, 2, NKEY)
        kaT = view(B, 34 * KB, 4, NKEY)
        w_abo = view(B, 0, KC, D)
        qsT = view(B, 0, 8, MT * P)
        ksT = view(B, 20 * KB, 4, NKEY)
        vs = view(B, 32 * KB, KT, 256)
        wg = [view(B, s * 24 * KB, KC, F) for s in range(2)]
        wu = [view(B, s * 24 * KB + 8 * KB, KC, F) for s in range(2)]
        wd = [view(B, s * 24 * KB + 16 * KB, 2, D) for s in range(2)]
        yc = [view(B, i * 4 * KB, D) for i in range(2 * MT)]
        radd = [view(ST, i * P, P) for i in range(2)]
        rmul = [view(ST, (2 + i) * P, P) for i in range(2)]
        arow = [view(ST, (4 + i) * P, P) for i in range(2)]
        acol = [view(ST, (6 + i) * P, 96) for i in range(2)]
        ada_out = [[view(A, KC * AB_IN + i * 512, 512) for i in range(2)], [view(ST, 8 * KB + i * 512, 512) for i in range(2)]]
        junk = view(ST, 4 * KB, D)
        qrow = view(ST, 0, 512)
        krow = view(ST, 2 * KB, 512)
        rtmp = view(ST, 4 * KB, 512)
        rtmp2 = view(ST, 6 * KB, 512)
        qlrow = view(ST, 8 * KB, QL)
        cvrow = view(ST, 8 * KB + QL, CKV + KR)
        qbrow = [view(ST, 0, 768), view(ST, 8 * KB, 768)]
        qsrow = view(ST, 0, D)
        ksrow = view(ST, 8 * KB, 4, 2, 64)
        prow = [view(ST, i * SW, SW) for i in range(3)]
        pT = [view(ST, 3 * SW + i * SW, MT, P) for i in range(2)]
        gate = [view(G, i * D, D) for i in range(2)]
        xn = [gate, [view(ST, 0, D), view(ST, 8 * KB, D)]]
        bc = [view(A, at * KB, 4, D) for at in (56, 0)]
        xg = [[view(A, at * KB + i * D, D) for i in range(2)] for at in (72, 16)]
        xgT = [[view(A, at * KB + i * D, KC, P) for i in range(2)] for at in (48, 24)]
        yr = [view(H, i * D, D) for i in range(2)]
        aT = [view(H, 8 * KB + i * 2 * P, 2 * P) for i in range(2)]
        ebuf = [view(H, 10 * KB + i * 2 * P, 2 * P) for i in range(2)]
        slot_lo = view(H, 0, 2 * MT, P)
        hit = view(H, 5 * KB, NT, E)
        slot_ge, slot_hi = view(H, 5 * KB + NT * E, 2 * MT, NT), view(H, 8 * KB, 2 * MT, NT)
        slotf, slotd, slotn = (view(H, 10 * KB + i * 2 * MT, 2 * MT) for i in range(3))
        rt = [12 * KB]

        def route_tmp(*dims):
            at = rt[0]
            rt[0] += int(np.prod(dims))
            assert rt[0] <= 20 * KB
            return view(H, at, *dims)

        sel, prod, o1, o2, mask = (route_tmp(MT, NG, EPG) for _ in range(5))
        pairs = route_tmp(MT * NG, 6)
        gs, goh, ing, ing2, oh1, oh2, eqt = (route_tmp(MT, 4) for _ in range(7))
        mx5 = route_tmp(MT)
        tot, cum, pref, slot = (route_tmp(MT, E) for _ in range(4))
        cnt, ntile, ends, starts = (route_tmp(E) for _ in range(4))
        thr_hit = route_tmp(E, MT)
        le_hit = route_tmp(E, E)
        cache_k = sb("cache_k_rows", [P, 512])
        cache_c = view(ST, 8 * KB + QL + CKV + KR, CKV + KR)
        sqj = sb("square_out", [P, 384])
        first_half = sqj[:, 0:P]
        ckv_g = sb("ckv_g", [P, CKV])
        ada_cols = [sb(f"ada_cols{l}", [P, 96]) for l in range(2)]
        cin = sb("cond_in", [P, 2, KC])
        cex = sb("cond_exp", [P, 2, KC])
        csil = sb("cond_silu", [P, 2, KC])
        gcols = sb("gain_cols", [P, 4])
        rw = sb("router_w_sb", [P, KC, E])
        rbias = sb("router_bias_sb", [P, E])
        sink8 = sb("sink8", [P, 16])
        lam = sb("lam", [P, 8])
        ss = sb("sum_squares", [P, 16])
        var = sb("variance", [P, 16])
        rstd = sb("rstd", [P, 16])
        mhalf = sb("minus_half", [P, 16])
        nmx = sb("neg_max", [P, 4])
        mxs = sb("row_max", [P, 4])
        rsum = sb("row_sum", [P, 4])
        rrec = sb("row_rec", [P, 4])
        orow = sb("head_rows", [P, 2, P])
        osq = sb("head_squares", [P, P])
        scores = sb("scores", [P, MT, E])
        wsel = sb("wsel", [P, 4, MT])
        slots = sb("slots", [P, 2, MT], I32)
        eidf = sb("eid_f", [P, NT])
        eidi = sb("eid_i", [P, NT], I32)
        idall = sb("slot_ids", [P, NT], I32)
        idt = [sb(f"slot_ids_now{i}", [P, 1], I32) for i in range(2)]

        ada_rows = scratch("ada_rows", [2, 2, 6 * D])
        h2_dram = scratch("h2_rows", [MT * P, D])
        y_dram = scratch("expert_rows", [NT * P, D])

        ld_cst, ld_c, ld_x, ld_x2, ld_small, ld_mod = (sem(n) for n in ("ld_cst", "ld_c", "ld_x", "ld_x2", "ld_small", "ld_mod"))
        ld_ada = [sem(f"ld_ada{i}") for i in range(3)]
        ld_win, ld_lat, ld_cache, ld_vcache = (sem(n) for n in ("ld_win", "ld_lat", "ld_cache", "ld_vcache"))
        units = [attention_units(l) for l in range(2)]
        UNITS = len(units[0])
        assert UNITS == len(units[1])

        def wide(l, n):
            return sum(len(u[3]) == 5 for u in units[l][:n])

        T_AFTER, V_AFTER, X_AFTER = 2, 3, 5

        def due(i, after):
            u = i - after
            return [u] if 0 <= u < UNITS and (after != X_AFTER or u % 2) else []

        ld_wout = Repeated("ld_wout", 16)
        ld_gate = Repeated("ld_gate", 32)
        ld_gate2 = Repeated("ld_gate2", 32)
        ld_bc = Repeated("ld_bc", 64)
        s_ss = Repeated("s_ss", MT)
        s_var = Repeated("s_var", MT)
        s_rstd = Repeated("s_rstd", MT)
        s_xn = Repeated("s_xn", MT)
        s_n1t = Repeated("s_n1t", MT)
        s_n1a = Repeated("s_n1a", MT)
        s_n1d = Repeated("s_n1d", MT)
        s_s = Repeated("s_scores", UNITS)
        s_nm = Repeated("s_negmax", UNITS)
        s_p = Repeated("s_probs", UNITS)
        s_t = Repeated("s_probsT", UNITS)
        s_ta = Repeated("s_pTa", UNITS)
        s_td = Repeated("s_pTd", wide(0, UNITS))
        s_o = Repeated("s_pv", UNITS)
        s_oe = Repeated("s_oevac", UNITS)
        s_or = Repeated("s_orow", UNITS // 2)
        s_ovar = Repeated("s_ovar", 4 * MT)
        s_orstd = Repeated("s_orstd", 4 * MT)
        s_x = Repeated("s_mixT", UNITS // 2)
        s_xe = Repeated("s_mixed", UNITS // 2)
        s_op = Repeated("s_outproj", 2 * MT)
        s_oped = Repeated("s_outevac", 2 * MT)
        s_xup = Repeated("s_xup", MT)
        s_n2ss = Repeated("s_n2ss", MT)
        s_n2var = Repeated("s_n2var", MT)
        s_n2r = Repeated("s_n2r", MT)
        s_h2 = Repeated("s_h2", MT)
        s_n2t = Repeated("s_n2t", MT)
        s_n2a = Repeated("s_n2a", MT)
        s_n2d = Repeated("s_n2d", MT)
        s_h2st = [Repeated(f"s_h2st{b}", 16 * (3 - b)) for b in range(2)]
        s_rt = Repeated("s_router", MT)
        s_rx = Repeated("s_rexp", MT)
        s_mask = Repeated("s_mask", 1)
        s_cnt = Repeated("s_count", 1)
        s_slots = Repeated("s_slots", 1)
        s_ya = Repeated("s_firstweighted", MT)
        s_oneh = Repeated("s_onehots", 1)
        s_idt = Repeated("s_idT", 1)
        s_ids = Repeated("s_ids", 1)
        ld_wswa, ld_scache, ld_fg = (sem(n) for n in ("ld_wswa", "ld_scache", "ld_fg"))
        s_filled = sem("s_filled")
        s_adaev, s_adatr = sem("s_adaev"), sem("s_adatr")
        s_cexp, s_csil, s_adamm, s_adac, s_adat, s_adar, s_adast, s_adat2, s_adacol = (
            sem(n) for n in ("s_cexp", "s_csil", "s_adamm", "s_adac", "s_adat", "s_adar", "s_adast", "s_adat2", "s_adacol"))
        s_lamx, s_lamp = sem("s_lamx"), sem("s_lamp")
        s_abp, s_aba, s_abd, s_abss, s_abvar, s_abr, s_abrow, s_abt, s_abta, s_abtd, s_about = (
            sem(n) for n in ("s_abp", "s_aba", "s_abd", "s_abss", "s_abvar", "s_abr", "s_abrow", "s_abt", "s_abta",
                             "s_abtd", "s_about"))
        s_qbp, s_qba, s_qbr, s_qbt, s_qbta, s_qbtd = (
            sem(n) for n in ("s_qbp", "s_qba", "s_qbr", "s_qbt", "s_qbta", "s_qbtd"))
        s_kvp, s_kva, s_kvd, s_krc = (sem(n) for n in ("s_kvp", "s_kva", "s_kvd", "s_krc"))
        s_swp, s_swd, s_swrow, s_swt, s_swta, s_swtd, s_swout = (
            sem(n) for n in ("s_swp", "s_swd", "s_swrow", "s_swt", "s_swta", "s_swtd", "s_swout"))
        s_mt, s_gu, s_dn, s_xea, s_xed, s_ex, s_mc, s_act, s_yea, s_yed, s_idc, s_comb = (
            per_layer(n) for n in ("s_moeT", "s_gateup", "s_down", "s_xTa", "s_xTd", "s_moeexp", "s_moechain",
                                   "s_moeact", "s_yea", "s_yed", "s_idcopy", "s_combined"))
        s_xg = [[sem(f"s_xg{b}_l{l}") for b in range(2)] for l in range(2)]
        s_wgu = [[sem(f"s_wgu{b}_l{l}") for b in range(2)] for l in range(2)]
        s_wd = [[sem(f"s_wd{b}_l{l}") for b in range(2)] for l in range(2)]
        s_yw = [[sem(f"s_yw{b}_l{l}") for b in range(2)] for l in range(2)]
        s_yc = [Repeated(f"s_yc{m}", 32) for m in range(MT)]
        s_fss, s_fvar, s_fr, s_fy, s_fout = (sem(n) for n in ("s_fss", "s_fvar", "s_fr", "s_fy", "s_fout"))
        chain_d = sem("dve_chain")
        s_idseen = sem("s_idseen")

        NP = NT // 2
        assert NT % 2 == 1
        AB_ORDER = [3, 4, 0, 1, 2]
        AB_COLS = [(0, 512), (512, 512), (1024, 512), (1536, QL), (1536 + QL, CKV + KR)]
        scale_of = {"diff": 64 ** -0.5, "mla": MQ ** -0.5, "swa": 64 ** -0.5}

        def cond(m):
            return 1 if m == PROMPT else 0

        def acolumn(l, m, j, k):
            at = cond(m) * 48 + j * 8 + k
            return ada_cols[l][:, at:at + 1]

        def tile_of(ap, m):
            return ap[:, m * P:(m + 1) * P]

        def q_of(l, u):
            kind, m, h, _ = u
            half = slice((h % 2) * 64, (h % 2) * 64 + 64)
            if kind == "mla":
                return qbT[0:MQ, h, m * P:(m + 1) * P]
            return (qaT if kind == "diff" else qsT)[half, h // 2, m * P:(m + 1) * P]

        def k_of(l, u, kt, n):
            kind, m, h, _ = u
            half = slice((h % 2) * 64, (h % 2) * 64 + 64)
            cols = slice(kt * P, (kt + n) * P)
            if kind == "mla":
                return kbT[0:MQ, h, cols]
            return kaT[half, h // 2, cols] if kind == "diff" else ksT[half, h // 4, cols]

        def v_of(l, u, kt):
            kind, m, h, _ = u
            if kind == "diff":
                return vd[:, kt, (h // 2) * P:(h // 2 + 1) * P]
            return vb[:, kt, h * 64:(h + 1) * 64] if kind == "mla" else vs[:, kt, (h // 4) * 64:(h // 4 + 1) * 64]

        def score_row(u, w):
            return ps[:, 2 * (u % 3):2 * (u % 3) + 2, :].rearrange("p a b -> p (a b)")[:, 0:w]

        def probs_t(u, j):
            return ps[:, 6, j * P:(j + 1) * P] if j < 4 else ps[:, 2 * (u % 3) + 1, P:2 * P]

        def v_width(u):
            return P if u[0] == "diff" else 64

        def row_bc(ap):
            return ap.to_broadcast([P, ap.shape[-1]])

        ada_src = ada_w.rearrange("l (p k) n -> l p k n", k=KC)
        kp = "(k p) n -> p k n"

        block = ctx.enter_context(nc.Block())

        @block.sync
        def _(sp):
            sp.dma_start(cin[:, 0, :], c_s.rearrange("a (p k) -> p (a k)", k=KC)).then_inc(ld_c, 16)
            sp.dma_start(cin[:, 1, :], c_ctx.rearrange("(p k) -> p k", k=KC)).then_inc(ld_c, 16)

            def ada_addends(l):
                for q in range(2):
                    sp.dma_start(radd[l][48 * q:48 * q + 48, :], ada_b[l].rearrange("(j p) -> j p", p=P)).then_inc(ld_mod, 16)
                    for j, n, g in ((0, 1, None), (1, 1, norm1_g), (2, 2, None), (4, 1, norm2_g), (5, 1, None)):
                        at = 48 * q + 8 * j
                        src = consts[0:8 * n, C_ONE:C_ONE + P] if g is None else g[l].rearrange("(j p) -> j p", p=P)
                        sp.dma_start(rmul[l][at:at + 8 * n, :], src).then_inc(ld_mod, 16)

            def ada_weights(l, first, end):
                for i in range(12 * l + first, 12 * l + end):
                    if i >= 3:
                        sp.wait_ge(s_adamm, i - 2)
                    sp.dma_start(ada_ring[l][i % 3], ada_src[l][:, :, (i - 12 * l) * 512:(i - 12 * l + 1) * 512])\
                        .then_inc(ld_ada[i % 3], 16)

            ada_weights(0, 0, 1)
            sp.dma_start(cst[:], consts).then_inc(ld_cst, 16)
            ada_weights(0, 1, 3)
            sp.dma_start(x_rows[:, 0:4, :], x_sample.rearrange("a (m p) d -> p (a m) d", p=P)).then_inc(ld_x, 16)
            sp.dma_start(x_rows[:, 4, :], x_prompt.rearrange("a p d -> p (a d)")).then_inc(ld_x, 16)
            ada_addends(0)
            ada_weights(0, 3, 12)
            sp.wait_ge(s_adamm, 12)
            sp.dma_start(wqb, mla_w_qb[0].rearrange(kp, p=P)).then_inc(ld_lat, 16)
            for k in range(2):
                for t in range(2):
                    sp.dma_start(wkvb[:, k, t * 512:(t + 1) * 512].rearrange("p (h d) -> p h d", d=64),
                                 mla_w_kvb[0, k * P:(k + 1) * P, :].rearrange("p (h t d) -> p h t d", t=2, d=64)[:, :, t, :])\
                        .then_inc(ld_lat, 16)
            sp.wait_ge(s_n1t.sem, s_n1t.at(0, MT))
            sp.dma_start(vd[:, CACHE_KT, :], cache_diff_v.rearrange("a b s h d -> s (a b h d)")).then_inc(ld_vcache, 16)
            sp.wait_ge(s_adar, 1)
            sp.dma_start(ada_rows[0].rearrange("q (j p) -> (q j) p", p=P), arow[0][0:96, :]).then_inc(s_adast, 16)
            sp.wait_ge(s_adast, 16)

            def load_rows(dst, l, j, s):
                for q in range(2):
                    sp.dma_start(dst[q], row_bc(ada_rows[l, q:q + 1, j * D:(j + 1) * D])).then_inc(s, 16)

            load_rows(gate, 0, 2, ld_gate.sem)
            sp.wait_ge(s_abrow, MT)
            sp.wait_ge(s_aba, 3 * MT)
            sp.wait_ge(s_abd, 2 * MT)
            sp.dma_start(new_diff_k.rearrange("a b s h t d -> s (a b h t d)"), krow).then_inc(s_about, 16)
            sp.dma_start(new_diff_v.rearrange("a b s h d -> s (a b h d)"), vd[:, PROMPT_KT, :]).then_inc(s_about, 16)
            sp.dma_start(new_mla_ckv.rearrange("a b s d -> s (a b d)"), cvrow[:, 0:CKV]).then_inc(s_about, 16)
            sp.dma_start(new_mla_krope.rearrange("a b s d -> s (a b d)"), cvrow[:, CKV:]).then_inc(s_about, 16)
            sp.wait_ge(s_kvp, 14)
            sp.wait_ge(s_krc, 8)
            sp.dma_start(w_abo, ab_w_out[0].rearrange(kp, p=P)).then_inc(ld_wout.sem, 16)
            sp.wait_ge(s_about, 64)
            sp.wait_ge(s_o.sem, s_o.at(0, 8 * MT))
            sp.dma_start(x_rows[:, 0:4, :], x_sample.rearrange("a (m p) d -> p (a m) d", p=P)).then_inc(ld_x2, 16)
            sp.dma_start(x_rows[:, 4, :], x_prompt.rearrange("a p d -> p (a d)")).then_inc(ld_x2, 16)

            for l in range(2):
                if l == 0:
                    for w, j in enumerate((4, 3)):
                        load_rows([bc[0][:, 2 * w, :], bc[0][:, 2 * w + 1, :]], 0, j, ld_bc.sem)
                    sp.wait_ge(s_s.sem, s_s.at(0, len(units[0])))
                    sp.wait_ge(s_o.sem, s_o.at(0, UNITS))
                    ada_weights(1, 0, 3)
                    ada_addends(1)
                else:
                    sp.wait_ge(s_comb[0], MT)
                    sp.dma_start(w_swao, swa_w_out[0].rearrange(kp, p=P)).then_inc(ld_wout.sem, 16)
                    for t in range(2):
                        sp.dma_start(cache_k.rearrange("p (h t d) -> p h t d", t=2, d=64)[:, :, t, :],
                                     cache_swa_k.rearrange("a b s h d -> s (a b h) d")).then_inc(ld_scache, 16)
                    sp.dma_start(vs[:, CACHE_KT, :], cache_swa_v.rearrange("a b s h d -> s (a b h d)")).then_inc(ld_scache, 16)
                    sp.wait_ge(s_n1t.sem, s_n1t.at(1, MT))
                    sp.wait_ge(s_adast, 32)
                    load_rows(gate, 1, 2, ld_gate.sem)
                    sp.wait_ge(s_swrow, MT)
                    sp.dma_start(new_swa_k.rearrange("a b s h d -> s (a b h) d"), ksrow[:, :, 0, :]).then_inc(s_swout, 16)
                    sp.dma_start(new_swa_v.rearrange("a b s h d -> s (a b h d)"), vs[:, PROMPT_KT, :]).then_inc(s_swout, 16)
                    sp.wait_ge(s_swp, 3 * MT)
                    for w, j in enumerate((4, 3)):
                        load_rows([bc[1][:, 2 * w, :], bc[1][:, 2 * w + 1, :]], 1, j, ld_bc.sem)
                    sp.wait_ge(s_swout, 32)
                for m in range(MT):
                    sp.wait_ge(s_h2.sem, s_h2.at(l, m + 1))
                    sp.dma_start(h2_dram[m * P:(m + 1) * P, :], xg[l][m % 2]).then_inc(s_h2st[m % 2].sem, 16)
                load_rows(gate, l, 5, ld_gate2.sem)
                if l == 0:
                    ada_weights(1, 3, 12)
                sp.wait_ge(s_slots.sem, s_slots.at(l, 1))
                sp.wait_ge(s_op.sem, s_op.at(l, 2 * MT))

                def expert_of(t):
                    return sp.value_load(eidi[0:1, bass.ds(t, 1)], min_val=0, max_val=E - 1)

                def weights(e, b, down):
                    todo = ((wd[b], moe_w_down),) if down else ((wg[b], moe_w_gate), (wu[b], moe_w_up))
                    for dst, src in todo:
                        sp.dma_start(dst, src[l][bass.ds(e, 1), :, :].rearrange("e (k p) n -> p (e k) n", p=P))\
                            .then_inc((s_wd if down else s_wgu)[l][b], 16)

                def expert_rows_out(i, b):
                    t = 2 * i + b
                    sp.wait_ge(s_yea[l], t + 3)
                    sp.wait_ge(s_yed[l], t + 3)
                    sp.dma_start(y_dram[bass.ds(t * P, P), :], yr[b]).then_inc(s_yw[l][b], 16)

                for b in range(2):
                    e = expert_of(b)
                    if b:
                        sp.wait_ge(s_idc[l], 2)
                    weights(e, b, False)
                    weights(e, b, True)

                def next_weights(i, b):
                    e = expert_of(2 * i + 2 + b)
                    sp.wait_ge(s_gu[l], 2 * i + b + 1)
                    weights(e, b, False)
                    sp.wait_ge(s_dn[l], 2 * i + b + 1)
                    weights(e, b, True)

                if l == 0:
                    sp.wait_ge(s_adamm, 24)
                    sp.dma_start(w_swa, swa_w_in[0].rearrange(kp, p=P)).then_inc(ld_wswa, 16)
                    sp.wait_ge(s_adar, 2)
                    sp.dma_start(ada_rows[1].rearrange("q (j p) -> (q j) p", p=P), arow[1][0:96, :]).then_inc(s_adast, 16)
                with sp.Fori(0, NP - 1) as i:
                    for b in range(2):
                        next_weights(i, b)
                        expert_rows_out(i, b)
                next_weights(NP - 1, 0)
                for b in range(2):
                    expert_rows_out(NP - 1, b)
                expert_rows_out(NP, 0)

            sp.wait_ge(s_swp, 3 * MT)
            sp.wait_ge(s_n2d.sem, s_n2d.at(1, MT))
            sp.wait_ge(s_h2.sem, s_h2.at(1, MT))
            sp.dma_start(bc[1][:, 0, :], row_bc(final_norm_g.rearrange("(a d) -> a d", a=1))).then_inc(ld_fg, 16)
            for m in range(MT):
                sp.wait_ge(s_fy, m + 1)
                dst = y_prompt.rearrange("a p d -> (a p) d") if m == PROMPT else \
                    y_sample.rearrange("a p d -> (a p) d")[m * P:(m + 1) * P, :]
                sp.dma_start(dst, x_rows[:, m, :]).then_inc(s_fout, 16)
            sp.wait_ge(s_fout, 16 * MT)

        @block.scalar
        def _(act):
            act.wait_ge(ld_c, 32)
            nc.scalar.activation(cex[:], cin[:], ACT.Exp, scale=-1.0).then_inc(s_cexp, 1)
            act.dma_start(sqj[:, 0:256], row_bc(diff_lambda.rearrange("l a d -> l (a d)"))).then_inc(ld_small, 16)
            act.dma_start(ckv_g[:], row_bc(mla_kv_norm_g)).then_inc(ld_small, 16)
            for k in range(3):
                act.dma_start(gcols[:, k:k + 1], mla_q_norm_g[0:1, k * P:(k + 1) * P].rearrange("a p -> p a"))\
                    .then_inc(ld_small, 16)
            act.dma_start(gcols[:, 3:4], diff_subln_g.rearrange("a p -> p a")).then_inc(ld_small, 16)
            act.dma_start(rw[:], router_w.rearrange("(k p) e -> p k e", p=P)).then_inc(ld_small, 16)
            act.dma_start(rbias[:], row_bc(router_bias.rearrange("(a e) -> a e", a=1))).then_inc(ld_small, 16)
            act.dma_start(sink8[:], row_bc(swa_sink)).then_inc(ld_small, 16)
            act.dma_start(cache_k[:], cache_diff_k.rearrange("a b s h t d -> s (a b h t d)")).then_inc(ld_cache, 16)
            act.dma_start(cache_c[:, 0:CKV], cache_mla_ckv.rearrange("a b s d -> s (a b d)")).then_inc(ld_cache, 16)
            act.dma_start(cache_c[:, CKV:], cache_mla_krope.rearrange("a b s d -> s (a b d)")).then_inc(ld_cache, 16)

            def square_sum(l, m):
                if m:
                    act.wait_ge(s_ss.sem, s_ss.at(l, m))
                nc.scalar.activation(junk, x_rows[:, m, :], ACT.Square, accum_out=ss[:, m:m + 1]).then_inc(s_ss.sem, 1)

            def norm1_evac(l, m):
                act.wait_ge(s_n1t.sem, s_n1t.at(l, m + 1))
                for k in range(4):
                    ins = nc.scalar.activation(hT[:, k, m * P:(m + 1) * P], ps[:, (m % 2) * 2, k * P:(k + 1) * P],
                                               ACT.Identity, scale=acolumn(l, m, 1, k), bias=acolumn(l, m, 0, k))
                ins.then_inc(s_n1a.sem, 1)

            def first_weighted(l, m):
                act.wait_ge(s_yc[m].sem, s_yc[m].at(l, 32))
                nc.scalar.activation(yc[2 * m], yc[2 * m], ACT.Copy, scale=wsel[:, 0, m:m + 1]).then_inc(s_ya.sem, 1)

            def ada_rows_out(l, first, end):
                for i in range(12 * l + first, 12 * l + end):
                    act.wait_ge(s_adamm, i + 1)
                    if i >= 2:
                        act.wait_ge(s_adatr, i - 1)
                    if 2 <= i < 6:
                        q = i - 2
                        act.dma_start(w_in[:, 2 * q:2 * q + 2, :], ab_w_in[0].rearrange(kp, p=P)[:, 2 * q:2 * q + 2, :])\
                            .then_inc(ld_win, 16)
                    nc.scalar.activation(ada_out[l][i % 2][0:2, :], ps[0:2, 4 + i % 2, :], ACT.Copy).then_inc(s_adaev, 1)

            ada_rows_out(0, 0, 6)
            act.wait_ge(s_lamp, 1)
            nc.scalar.activation(lam[:, 2:4], lam[:, 0:2], ACT.Exp).then_inc(s_lamx, 1)
            act.wait_ge(ld_x, 32)
            for m in range(MT):
                square_sum(0, m)
            ada_rows_out(0, 6, 12)
            act.wait_ge(s_adacol, 1)
            for m in range(MT):
                norm1_evac(0, m)

            act.wait_ge(ld_small, 9 * 16)

            def ab_transposed(m):
                act.wait_ge(s_abt, 4 * m + 2)
                kt = PROMPT_KT if m == PROMPT else m
                nc.scalar.activation(kaT[:, :, kt * P:(kt + 1) * P], ps[:, 1, :].rearrange("p (c t) -> p c t", c=4),
                                     ACT.Copy).then_inc(s_abta, 1)
                act.wait_ge(s_abt, 4 * m + 3)
                for k in range(3):
                    ins = nc.scalar.activation(qlT[:, k, m * P:(m + 1) * P], ps[:, 2, k * P:(k + 1) * P], ACT.Copy,
                                               scale=gcols[:, k:k + 1])
                ins.then_inc(s_abta, 1)

            for m in range(MT):
                n = 5 * m
                act.wait_ge(s_abp, n + 1)
                if m:
                    act.wait_ge(s_abss, 2 * m)
                nc.scalar.activation(sqj[:, 0:QL], ps[:, 4 + n % 4, 0:QL], ACT.Square, accum_out=ss[:, 8:9])\
                    .then_inc(s_abss, 1)
                act.wait_ge(s_abp, n + 2)
                act.wait_ge(s_abss, 2 * m + 1)
                nc.scalar.activation(sqj[:, 0:CKV], ps[:, 4 + (n + 1) % 4, 0:CKV], ACT.Square, accum_out=ss[:, 9:10])\
                    .then_inc(s_abss, 1)
                if m:
                    ab_transposed(m - 1)
                    act.wait_ge(s_abt, 4 * m)
                act.wait_ge(s_abr, m + 1)
                nc.scalar.activation(qlrow, ps[:, 4 + n % 4, 0:QL], ACT.Copy, scale=rstd[:, 8:9]).then_inc(s_aba, 1)
                nc.scalar.activation(cvrow[:, 0:CKV], ps[:, 4 + (n + 1) % 4, 0:CKV], ACT.Copy, scale=rstd[:, 9:10])
                nc.scalar.activation(cvrow[:, CKV:], ps[:, 4 + (n + 1) % 4, CKV:CKV + KR], ACT.Copy).then_inc(s_aba, 1)
                act.wait_ge(s_abp, n + 5)
                kt = PROMPT_KT if m == PROMPT else m
                nc.scalar.activation(vd[:, kt, :], ps[:, 4 + (n + 4) % 4, :], ACT.Copy).then_inc(s_aba, 1)
            ab_transposed(MT - 1)
            act.wait_ge(s_abt, 4 * MT + 1)
            nc.scalar.activation(kaT[:, :, CACHE_KT * P:(CACHE_KT + 1) * P], ps[:, 1, :].rearrange("p (c t) -> p c t", c=4),
                                 ACT.Copy).then_inc(s_abta, 1)

            act.wait_ge(s_about, 64)
            act.wait_ge(s_abt, 4 * MT + 2)

            def qb_transposed(m):
                act.wait_ge(s_qbt, 2 * m + 2)
                nc.scalar.activation(qbT[0:MQ, 4:8, m * P:(m + 1) * P],
                                     ps[0:MQ, (m % 2) * 2 + 1, :].rearrange("p (c t) -> p c t", c=4), ACT.Copy)\
                    .then_inc(s_qbta, 1)

            for j in range(2 * MT):
                m, half = divmod(j, 2)
                if m >= 2 and half == 0:
                    act.wait_ge(s_qbt, 2 * (m - 1))
                act.wait_ge(s_qbp, j + 1)
                nc.scalar.activation(qbrow[m % 2][:, half * 384:(half + 1) * 384], ps[:, 4 + j % 4, 0:384], ACT.Copy)\
                    .then_inc(s_qba, 1)
                if half and m:
                    qb_transposed(m - 1)
            qb_transposed(MT - 1)
            for kt in range(KT):
                act.wait_ge(s_kvp, 2 * kt + 1)
                nc.scalar.activation(vb[:, kt, :], ps[:, 4 + (2 * kt) % 4, :], ACT.Copy).then_inc(s_kva, 1)

            def attention(l):
                U = units[l]
                n = len(U)
                for i in range(n + 5):
                    for u in due(i, X_AFTER):
                        j = u // 2
                        kind, m, h, _ = U[2 * j]
                        chunk = h // 2 + (4 if kind == "mla" else 0)
                        act.wait_ge(s_x.sem, s_x.at(l, j + 1))
                        dst = hT[:, chunk, m * P:(m + 1) * P]
                        if kind == "diff":
                            ins = nc.scalar.activation(dst, ps[:, 7, P:2 * P], ACT.Copy, scale=lam[:, 5:6])
                        else:
                            ins = nc.scalar.activation(dst, ps[:, 7, P:2 * P], ACT.Copy)
                        ins.then_inc(s_xe.sem, 1)
                    for u in due(i, T_AFTER):
                        w = min(len(U[u][3]), 4)
                        act.wait_ge(s_t.sem, s_t.at(l, u + 1))
                        nc.scalar.activation(pT[u % 2][:, 0:w, :],
                                             ps[:, 6, 0:w * P].rearrange("p (c t) -> p c t", c=w), ACT.Copy)\
                            .then_inc(s_ta.sem, 1)
                    if i < n:
                        kind, m, h, kts = U[i]
                        w = len(kts) * P + (kind == "swa")
                        act.wait_ge(s_nm.sem, s_nm.at(l, i + 1))
                        if i >= 3:
                            act.wait_ge(s_t.sem, s_t.at(l, i - 2))
                        sc = score_row(i, w)
                        nc.scalar.activation(prow[i % 3][:, 0:w], sc, ACT.Exp, bias=nmx[:, i % 4:i % 4 + 1],
                                             scale=scale_of[kind], accum_out=rsum[:, i % 4:i % 4 + 1])\
                            .then_inc(s_p.sem, 1)

            def norm2(l):
                for m in range(MT + 3):
                    if m < MT:
                        act.wait_ge(s_xup.sem, s_xup.at(l, m + 1))
                        if m:
                            act.wait_ge(s_n2ss.sem, s_n2ss.at(l, m))
                        nc.scalar.activation(junk, x_rows[:, m, :], ACT.Square, accum_out=ss[:, m:m + 1])\
                            .then_inc(s_n2ss.sem, 1)
                    if 2 <= m <= MT + 1:
                        act.wait_ge(s_n2t.sem, s_n2t.at(l, m - 1))
                        nc.scalar.activation(xgT[l][m % 2][:, 0:4, :],
                                             ps[:, 4, :].rearrange("p (c t) -> p c t", c=4), ACT.Copy)\
                            .then_inc(s_n2a.sem, 1)
                    if m >= 3:
                        act.wait_ge(s_rt.sem, s_rt.at(l, m - 2))
                        nc.scalar.activation(scores[:, m - 3, :], ps[:, 6, 0:E], ACT.Exp, scale=-1.0)\
                            .then_inc(s_rx.sem, 1)

            def experts(l):
                def gathered(i, b):
                    t = 2 * i + b
                    act.wait_ge(s_mt[l], t + 1)
                    nc.scalar.activation(xgT[l][b][:, 0:4, :], ps[:, 0, :].rearrange("p (c t) -> p c t", c=4),
                                         ACT.Copy).then_inc(s_xea[l], 1)

                def silu(i, b):
                    t = 2 * i + b
                    act.wait_ge(s_gu[l], t + 1)
                    nc.scalar.activation(ebuf[b], ps[:, 2 + b, 0:2 * P], ACT.Exp, scale=-1.0).then_inc(s_ex[l], 1)

                def out_rows(i, b):
                    act.wait_ge(s_dn[l], 2 * i + b + 1)
                    act.wait_ge(s_yw[l][b], 16 * i + 16)
                    nc.scalar.activation(yr[b][:, 0:512], ps[:, 4 + 2 * b, :], ACT.Copy).then_inc(s_yea[l], 1)

                for b in range(2):
                    act.sem_inc(s_yw[l][b], 16)
                act.sem_inc(s_yea[l], 2)
                gathered(0, 0)
                silu(0, 0)
                gathered(0, 1)
                with act.Fori(0, NP - 1) as i:
                    silu(i, 1)
                    gathered(i + 1, 0)
                    out_rows(i, 0)
                    silu(i + 1, 0)
                    gathered(i + 1, 1)
                    out_rows(i, 1)
                silu(NP - 1, 1)
                gathered(NP, 0)
                out_rows(NP - 1, 0)
                silu(NP, 0)
                out_rows(NP - 1, 1)
                out_rows(NP, 0)

            attention(0)
            act.wait_ge(s_t.sem, s_t.at(0, UNITS))
            act.wait_ge(s_o.sem, s_o.at(0, UNITS))
            norm2(0)
            ada_rows_out(1, 0, 12)
            experts(0)
            for m in range(MT + 2):
                if m < MT:
                    first_weighted(0, m)
                if 1 <= m <= MT:
                    act.wait_ge(s_comb[0], m)
                    square_sum(1, m - 1)
                if m >= 2:
                    norm1_evac(1, m - 2)

            def sw_transposed(m, kt):
                if kt != CACHE_KT:
                    act.wait_ge(s_swt, 3 * m + 1)
                    nc.scalar.activation(qsT[:, 0:4, m * P:(m + 1) * P], ps[:, 0, :].rearrange("p (c t) -> p c t", c=4),
                                         ACT.Copy).then_inc(s_swta, 1)
                    act.wait_ge(s_swt, 3 * m + 3)
                else:
                    act.wait_ge(s_swt, 3 * MT + 1)
                nc.scalar.activation(ksT[:, :, kt * P:(kt + 1) * P], ps[:, 2, :].rearrange("p (c t) -> p c t", c=4),
                                     ACT.Copy).then_inc(s_swta, 1)

            for m in range(MT):
                sw_transposed(m, PROMPT_KT if m == PROMPT else m)
            sw_transposed(MT, CACHE_KT)
            act.wait_ge(s_swout, 32)
            act.wait_ge(s_swt, 3 * MT + 1)
            attention(1)
            act.wait_ge(s_t.sem, s_t.at(1, UNITS))
            act.wait_ge(s_o.sem, s_o.at(1, UNITS))
            norm2(1)
            experts(1)
            for m in range(MT + 1):
                if m < MT:
                    first_weighted(1, m)
                if m:
                    act.wait_ge(s_comb[1], m)
                    if m > 1:
                        act.wait_ge(s_fss, m - 1)
                    nc.scalar.activation(junk, x_rows[:, m - 1, :], ACT.Square, accum_out=ss[:, m - 1:m]).then_inc(s_fss, 1)

        @block.gpsimd
        def _(pool):
            nc.gpsimd.memset(mhalf[:], -0.5).then_inc(s_filled, 1)
            pool.wait_ge(s_filled, 1)

            def inverse_root(at, n, ready, value, done):
                pool.wait_ge(ready, value)
                nc.gpsimd.tensor_tensor(rstd[:, at:at + n], var[:, at:at + n], mhalf[:, at:at + n], ALU.pow)\
                    .then_inc(done, 1)

            def head_roots():
                for j in range(4 * MT):
                    inverse_root(12 + j % 2, 1, s_ovar.sem, j + 1, s_orstd.sem)

            def after_attention(l):
                for m in range(MT):
                    inverse_root(m, 1, s_n2var.sem, s_n2var.at(l, m + 1), s_n2r.sem)
                pool.wait_ge(s_ids.sem, s_ids.at(l, 1))
                for b in range(2):
                    pool.wait_ge(s_h2st[b].sem, s_h2st[b].at(l, 16 * (3 - b)))

                def gather(t, b, n):
                    nc.gpsimd.tensor_copy(idt[b][:], idall[:, bass.ds(t, 1)]).then_inc(s_idc[l], 1)
                    pool.wait_ge(s_idc[l], n)
                    pool.sem_inc(s_idseen, 1)
                    pool.indirect_dma_start(xg[l][b], None, h2_dram, bass.IndirectOffsetOnAxis(idt[b][:], 0))\
                        .then_inc(s_xg[l][b], 16)

                for b in range(2):
                    gather(b, b, b + 1)
                with pool.Fori(0, NP - 1) as i:
                    for b in range(2):
                        pool.wait_ge(s_mt[l], 2 * i + b + 1)
                        gather(2 * i + 2 + b, b, 2 * i + 3 + b)
                pool.wait_ge(s_mt[l], NT - 2)
                gather(NT - 1, 0, NT)
                for b in range(2):
                    pool.wait_ge(s_yw[l][b], 16 * (NP + 2 - b))
                for m in range(MT):
                    for w in range(2):
                        pool.indirect_dma_start(yc[2 * m + w], None, y_dram,
                                                bass.IndirectOffsetOnAxis(slots[:, w, m:m + 1], 0))\
                            .then_inc(s_yc[m].sem, 16)

            for m in range(MT):
                inverse_root(m, 1, s_var.sem, s_var.at(0, m + 1), s_rstd.sem)
            for m in range(MT):
                inverse_root(8, 2, s_abvar, m + 1, s_abr)
            pool.wait_ge(s_abtd, 2 * MT + 1)
            pool.wait_ge(s_abp, 5 * MT)
            for h in range(MH):
                nc.gpsimd.tensor_copy(kbT[64:96, h, :], krT[0:32, :]).then_inc(s_krc, 1)
            head_roots()
            after_attention(0)
            for m in range(MT):
                inverse_root(m, 1, s_var.sem, s_var.at(1, m + 1), s_rstd.sem)
            after_attention(1)
            for m in range(MT):
                inverse_root(m, 1, s_fvar, m + 1, s_fr)

        @block.vector
        def _(dve):
            steps = [0]

            def link(*instructions):
                for ins in instructions:
                    ins.then_inc(chain_d, 1)
                    steps[0] += 1
                dve.wait_ge(chain_d, steps[0])

            tt = nc.vector.tensor_tensor
            ts = nc.vector.tensor_scalar

            dve.wait_ge(s_cexp, 1)
            link(ts(cex[:], cex[:], 1.0, None, ALU.add))
            link(nc.vector.reciprocal(cex[:], cex[:]))
            tt(csil[:], cin[:], cex[:], ALU.mult).then_inc(s_csil, 1)
            dve.wait_ge(ld_small, 9 * 16)
            l4 = sqj[:, 0:256].rearrange("p (a b d) -> p a b d", a=2, b=2)
            link(tt(sqj[:, 256:384].rearrange("p (a d) -> p a d", a=2), l4[:, :, 0, :], l4[:, :, 1, :], ALU.mult))
            nc.vector.tensor_reduce(lam[:, 0:2], sqj[:, 256:384].rearrange("p (a d) -> p a d", a=2), AX_X, ALU.add)\
                .then_inc(s_lamp, 1)
            dve.wait_ge(s_lamx, 1)
            link(tt(lam[:, 4:5], lam[:, 3:4], lam[:, 2:3], ALU.subtract))
            link(ts(lam[:, 4:5], lam[:, 4:5], -LAMBDA_INIT, None, ALU.add))
            link(ts(lam[:, 5:6], gcols[:, 3:4], 1.0 - LAMBDA_INIT, None, ALU.mult))
            link(ts(sink8[:], sink8[:], 8.0, None, ALU.mult))

            def variance(at, n, width, *, out):
                ts(var[:, at:at + n], ss[:, at:at + n], 1.0 / width, EPS, ALU.mult, ALU.add).then_inc(out, 1)

            for m in range(MT):
                dve.wait_ge(s_ss.sem, s_ss.at(0, m + 1))
                variance(m, 1, D, out=s_var.sem)

            def ada(l):
                dve.wait_ge(s_adatr, 12 * (l + 1))
                nc.vector.tensor_copy(acol[l], ps[:, l, 0:96]).then_inc(s_adac, 1)
                dve.wait_ge(s_adat, l + 1)
                dve.wait_ge(ld_mod, 12 * 16 * (l + 1))
                dve.wait_ge(ld_cst, 16)
                link(nc.vector.scalar_tensor_tensor(out=arow[l][0:96, :], in0=ps[0:96, 2 + l, 0:P],
                                                    scalar=cst[0:96, C_SCL:C_SCL + 1], in1=radd[l][0:96, :],
                                                    op0=ALU.add, op1=ALU.add))
                tt(arow[l][0:96, :], arow[l][0:96, :], rmul[l][0:96, :], ALU.mult).then_inc(s_adar, 1)
                dve.wait_ge(s_adat2, l + 1)
                nc.vector.tensor_copy(ada_cols[l][:], ps[:, 4 + l, 0:96]).then_inc(s_adacol, 1)

            def normed(l, m):
                if m >= 2:
                    dve.wait_ge(s_n1t.sem, s_n1t.at(l, m - 1))
                dve.wait_ge(s_rstd.sem, s_rstd.at(l, m + 1))
                ts(xn[l][m % 2], x_rows[:, m, :], rstd[:, m:m + 1], None, ALU.mult).then_inc(s_xn.sem, 1)

            def norm1_evac(l, m):
                dve.wait_ge(s_n1t.sem, s_n1t.at(l, m + 1))
                for k in range(4, KC):
                    ins = ts(hT[:, k, m * P:(m + 1) * P], ps[:, (m % 2) * 2 + 1, (k - 4) * P:(k - 3) * P],
                             acolumn(l, m, 1, k), acolumn(l, m, 0, k), ALU.mult, ALU.add)
                ins.then_inc(s_n1d.sem, 1)

            ada(0)
            for m in range(MT + 1):
                if m < MT:
                    normed(0, m)
                if m:
                    norm1_evac(0, m - 1)
            dve.wait_ge(s_adast, 16)

            def rope(dst, src, m, dim, heads, done=None):
                def tab(c):
                    return cst[:, c + m * dim:c + (m + 1) * dim].unsqueeze(1).broadcast_to([P, heads, dim])
                co, si = tab(C_C64 if dim == 64 else C_C32), tab(C_S64 if dim == 64 else C_S32)
                n = heads * dim
                t = rtmp[:, 0:n].rearrange("p (h d) -> p h d", h=heads)
                t2 = rtmp2[:, 0:n].rearrange("p (h d) -> p h d", h=heads)
                link(tt(t, src, co, ALU.mult),
                     tt(t2[:, :, 0::2], src[:, :, 1::2], si[:, :, 0::2], ALU.mult),
                     tt(t2[:, :, 1::2], src[:, :, 0::2], si[:, :, 1::2], ALU.mult))
                return tt(dst, t, t2, ALU.add)

            def ab_transposed(m):
                dve.wait_ge(s_abt, 4 * m + 1)
                nc.vector.tensor_copy(qaT[:, :, m * P:(m + 1) * P], ps[:, 0, :].rearrange("p (c t) -> p c t", c=4))
                latents_transposed(PROMPT_KT if m == PROMPT else m, 4 * m + 4)

            def latents_transposed(kt, n):
                dve.wait_ge(s_abt, n)
                nc.vector.tensor_copy(ckvT[:, :, kt * P:(kt + 1) * P], ps[:, 3, 0:2 * P].rearrange("p (c t) -> p c t", c=2))
                nc.vector.tensor_copy(krT[0:KR, kt * P:(kt + 1) * P], ps[0:KR, 3, 2 * P:3 * P]).then_inc(s_abtd, 2 if n % 4 == 0 else 1)

            for m in range(MT):
                n = 5 * m
                dve.wait_ge(s_abss, 2 * m + 2)
                ts(var[:, 8:9], ss[:, 8:9], 1.0 / QL, EPS, ALU.mult, ALU.add)
                ts(var[:, 9:10], ss[:, 9:10], 1.0 / CKV, EPS, ALU.mult, ALU.add).then_inc(s_abvar, 1)
                if m:
                    ab_transposed(m - 1)
                for o, row in ((0, qrow), (1, krow)):
                    dve.wait_ge(s_abp, n + 3 + o)
                    if m and o == 0:
                        dve.wait_ge(s_abrow, m)
                    src = ps[:, 4 + (n + 2 + o) % 4, :]
                    if m == PROMPT:
                        ins = nc.vector.tensor_copy(row, src)
                    else:
                        v = "p (h d) -> p h d"
                        ins = rope(row.rearrange(v, d=64), src.rearrange(v, d=64), m, 64, 8)
                    link(ins)
                    dve.sem_inc(s_abd, 1)
                dve.wait_ge(s_aba, 3 * m + 2)
                if m == PROMPT:
                    tt(cvrow[:, 0:CKV], cvrow[:, 0:CKV], ckv_g[:], ALU.mult).then_inc(s_abrow, 1)
                else:
                    link(tt(cvrow[:, 0:CKV], cvrow[:, 0:CKV], ckv_g[:], ALU.mult))
                    kr = cvrow[:, CKV:].unsqueeze(1)
                    rope(kr, kr, m, 32, 1).then_inc(s_abrow, 1)
            ab_transposed(MT - 1)
            latents_transposed(CACHE_KT, 4 * MT + 2)

            def qb_transposed(m):
                dve.wait_ge(s_qbt, 2 * m + 1)
                nc.vector.tensor_copy(qbT[0:MQ, 0:4, m * P:(m + 1) * P],
                                      ps[0:MQ, (m % 2) * 2, :].rearrange("p (c t) -> p c t", c=4)).then_inc(s_qbtd, 1)

            for m in range(MT):
                dve.wait_ge(s_qba, 2 * m + 2)
                if m < PROMPT:
                    if m:
                        dve.wait_ge(s_qbr, m)
                    v = qbrow[m % 2].rearrange("p (h d) -> p h d", h=MH)[:, :, NOPE:]
                    rope(v, v, m, 32, MH).then_inc(s_qbr, 1)
                else:
                    dve.wait_ge(s_qbr, m)
                    dve.sem_inc(s_qbr, 1)
                if m:
                    qb_transposed(m - 1)
            qb_transposed(MT - 1)
            for i in range(8):
                n = 2 * i + 1 if i < 6 else 6 + i
                p, piece = divmod(i, 2)
                cols = slice(0, 512) if piece == 0 else slice(512, NKEY)
                w = 512 if piece == 0 else NKEY - 512
                dve.wait_ge(s_kvp, n + 1)
                nc.vector.tensor_copy(kbT[0:64, 2 * p, cols], ps[0:64, 4 + n % 4, 0:w])
                nc.vector.tensor_copy(kbT[0:64, 2 * p + 1, cols], ps[64:128, 4 + n % 4, 0:w]).then_inc(s_kvd, 1)

            def attention(l):
                U = units[l]
                n = len(U)

                def rows_out(u):
                    kind, m, h, _ = U[u]
                    j = u // 2
                    col = slice(u % 4, u % 4 + 1)
                    dve.wait_ge(s_o.sem, s_o.at(l, u + 1))
                    if j >= 2 and u % 2 == 0:
                        dve.wait_ge(s_x.sem, s_x.at(l, j - 1))
                    link(nc.vector.reciprocal(rrec[:, col], rsum[:, col]))
                    if kind == "diff" and u % 2 == 0:
                        ts(first_half, ps[:, 7, 0:P], rrec[:, col], None, ALU.mult).then_inc(s_oe.sem, 1)
                    elif kind == "diff":
                        link(ts(rrec[:, col], rrec[:, col], lam[:, 4:5], None, ALU.mult))
                        dve.wait_ge(s_oe.sem, s_oe.at(l, u))
                        nc.vector.scalar_tensor_tensor(out=orow[:, j % 2, :], in0=ps[:, 7, 0:P], scalar=rrec[:, col],
                                                       in1=first_half, op0=ALU.mult, op1=ALU.add).then_inc(s_oe.sem, 1)
                        dve.wait_ge(s_oe.sem, s_oe.at(l, u + 1))
                        link(nc.vector.tensor_tensor_reduce(out=osq[:], in0=orow[:, j % 2, :], in1=orow[:, j % 2, :],
                                                            scale=1.0, scalar=0.0, op0=ALU.mult, op1=ALU.add,
                                                            accum_out=ss[:, 12 + j % 2:13 + j % 2]))
                        variance(12 + j % 2, 1, P, out=s_ovar.sem)
                    else:
                        half = slice((u % 2) * 64, (u % 2) * 64 + 64)
                        ts(orow[:, j % 2, half], ps[:, 7, 0:64], rrec[:, col], None, ALU.mult).then_inc(s_oe.sem, 1)
                        if u % 2:
                            dve.wait_ge(s_oe.sem, s_oe.at(l, u + 1))
                            if l or j:
                                dve.wait_ge(s_or.sem, s_or.at(l, j))
                            dve.sem_inc(s_or.sem, 1)

                for i in range(n + 3):
                    if i < n:
                        kind, m, h, kts = U[i]
                        w = len(kts) * P
                        dve.wait_ge(s_s.sem, s_s.at(l, i + 1))
                        sc = score_row(i, SW)
                        if kind == "swa":
                            todo = []
                            if m != PROMPT:
                                for j, kt in enumerate(kts[:-1]):
                                    if kt != m:
                                        s = sc[:, j * P:(j + 1) * P]
                                        todo.append(tt(s, s, masks[kt - m], ALU.add))
                            todo.append(nc.vector.tensor_copy(sc[:, w:w + 1], sink8[:, h:h + 1]))
                            link(*todo)
                            w += 1
                        link(nc.vector.tensor_reduce(mxs[:, i % 4:i % 4 + 1], sc[:, 0:w], AX_X, ALU.max))
                        ts(nmx[:, i % 4:i % 4 + 1], mxs[:, i % 4:i % 4 + 1], -scale_of[kind], None, ALU.mult)\
                            .then_inc(s_nm.sem, 1)
                    if i >= 5 and i % 2 and U[i - 5][0] == "diff":
                        j = (i - 5) // 2
                        dve.wait_ge(s_orstd.sem, s_orstd.at(l, j + 1))
                        ts(orow[:, j % 2, :], orow[:, j % 2, :], rstd[:, 12 + j % 2:13 + j % 2], None, ALU.mult)\
                            .then_inc(s_or.sem, 1)
                    for u in due(i, T_AFTER):
                        if len(U[u][3]) == 5:
                            dve.wait_ge(s_t.sem, s_t.at(l, u + 1))
                            nc.vector.tensor_copy(pT[u % 2][:, 4, :], probs_t(u, 4)).then_inc(s_td.sem, 1)
                    for u in due(i, V_AFTER):
                        rows_out(u)

            def out_and_norm2(l):
                dve.wait_ge(ld_gate.sem, ld_gate.at(l, 32))
                if l == 0:
                    dve.wait_ge(ld_x2, 32)
                dve.wait_ge(ld_bc.sem, ld_bc.at(l, 64))
                for m in range(MT + 2):
                    if m < MT:
                        for half in range(2):
                            j = 2 * m + half
                            cols = slice(half * 512, half * 512 + 512)
                            dve.wait_ge(s_op.sem, s_op.at(l, j + 1))
                            t = (prow_a, prow_b)[half]
                            tt(t, ps[:, j % 4, :], gate[cond(m)][:, cols], ALU.mult).then_inc(s_oped.sem, 1)
                            dve.wait_ge(s_oped.sem, s_oped.at(l, j + 1))
                            ins = tt(x_rows[:, m, cols], x_rows[:, m, cols], t, ALU.add)
                        ins.then_inc(s_xup.sem, 1)
                    if 1 <= m <= MT:
                        u = m - 1
                        dve.wait_ge(s_n2ss.sem, s_n2ss.at(l, u + 1))
                        variance(u, 1, D, out=s_n2var.sem)
                        if u >= 2:
                            dve.wait_ge(s_h2st[u % 2].sem, s_h2st[u % 2].at(l, 16 * (u // 2)))
                            dve.wait_ge(s_n2t.sem, s_n2t.at(l, u - 1))
                        dve.wait_ge(s_n2r.sem, s_n2r.at(l, u + 1))
                        h2 = xg[l][u % 2]
                        link(nc.vector.scalar_tensor_tensor(out=h2, in0=x_rows[:, u, :], scalar=rstd[:, u:u + 1],
                                                            in1=bc[l][:, cond(u), :], op0=ALU.mult, op1=ALU.mult))
                        tt(h2, h2, bc[l][:, 2 + cond(u), :], ALU.add).then_inc(s_h2.sem, 1)
                    if m >= 2:
                        u = m - 2
                        dve.wait_ge(s_n2t.sem, s_n2t.at(l, u + 1))
                        nc.vector.tensor_copy(xgT[l][u % 2][:, 4:8, :], ps[:, 5, :].rearrange("p (c t) -> p c t", c=4))\
                            .then_inc(s_n2d.sem, 1)

            def first_of(v, out):
                m4 = mx5.unsqueeze(2).broadcast_to([P, MT, 4])
                code = cst[:, C_CODE:C_CODE + 4].unsqueeze(1).broadcast_to([P, MT, 4])
                link(nc.vector.tensor_reduce(mx5, v, AX_X, ALU.max))
                link(tt(eqt, v, m4, ALU.is_equal))
                link(tt(eqt, eqt, code, ALU.mult))
                link(nc.vector.tensor_reduce(mx5, eqt, AX_X, ALU.max))
                link(tt(out, eqt, m4, ALU.is_equal))

            def route(l):
                sc4 = scores[:].rearrange("p m (g e) -> p m g e", g=NG)
                dve.wait_ge(s_rx.sem, s_rx.at(l, MT))
                link(ts(scores[:], scores[:], 1.0, None, ALU.add))
                link(nc.vector.reciprocal(scores[:], scores[:]))
                link(tt(sel.rearrange("p m g e -> p m (g e)"), scores[:], rbias[:].unsqueeze(1).broadcast_to([P, MT, E]), ALU.add))
                s20 = sel.rearrange("p m g e -> p (m g) e")
                link(tt(pairs[:, :, 0:3], s20[:, :, 0:3], s20[:, :, 1:4], ALU.add),
                     tt(pairs[:, :, 3:5], s20[:, :, 0:2], s20[:, :, 2:4], ALU.add),
                     tt(pairs[:, :, 5:6], s20[:, :, 0:1], s20[:, :, 3:4], ALU.add))
                link(nc.vector.tensor_reduce(gs.rearrange("p m g -> p (m g)"), pairs, AX_X, ALU.max))
                first_of(gs, goh)
                link(tt(prod, sel, goh.unsqueeze(3).broadcast_to([P, MT, NG, EPG]), ALU.mult))
                link(nc.vector.tensor_reduce(ing, prod.rearrange("p m g e -> p m e g"), AX_X, ALU.add))
                first_of(ing, oh1)
                link(nc.vector.scalar_tensor_tensor(out=ing2, in0=oh1, scalar=NEG, in1=ing, op0=ALU.mult, op1=ALU.add))
                first_of(ing2, oh2)
                for o, oh in ((o1, oh1), (o2, oh2)):
                    link(tt(o, goh.unsqueeze(3).broadcast_to([P, MT, NG, EPG]),
                            oh.unsqueeze(2).broadcast_to([P, MT, NG, EPG]), ALU.mult))
                tt(mask, o1, o2, ALU.add).then_inc(s_mask.sem, 1)
                dve.wait_ge(s_cnt.sem, s_cnt.at(l, 1))
                v = "p (m e) -> p m e"
                link(nc.vector.tensor_copy(cum, ps[:, 7, 0:80].rearrange(v, e=E)),
                     nc.vector.tensor_copy(tot, ps[:, 7, 80:160].rearrange(v, e=E)),
                     nc.vector.memset(pref[:, 0, :], 0.0))
                for m in range(1, MT):
                    link(tt(pref[:, m, :], pref[:, m - 1, :], tot[:, m - 1, :], ALU.add))
                link(tt(cnt, pref[:, MT - 1, :], tot[:, MT - 1, :], ALU.add))
                link(tt(cum, cum, pref, ALU.add))
                link(tt(thr_hit, cnt.unsqueeze(2).broadcast_to([P, E, MT]),
                        cst[:, C_THR:C_THR + 80].rearrange("p (e k) -> p e k", e=E), ALU.is_gt))
                link(nc.vector.tensor_reduce(ntile, thr_hit, AX_X, ALU.add))
                link(tt(le_hit, ntile.unsqueeze(1).broadcast_to([P, E, E]),
                        cst[:, C_LE:C_LE + E * E].rearrange("p (e k) -> p e k", e=E), ALU.mult))
                link(nc.vector.tensor_reduce(ends, le_hit, AX_X, ALU.add))
                link(tt(hit, ends.unsqueeze(1).broadcast_to([P, NT, E]),
                        cst[:, C_IOTA:C_IOTA + NT * E].rearrange("p (t e) -> p t e", e=E), ALU.is_le))
                link(nc.vector.tensor_reduce(eidf[:], hit, AX_X, ALU.add))
                link(ts(eidf[:], eidf[:], float(E - 1), None, ALU.min))
                nc.vector.tensor_copy(eidi[:], eidf[:]).then_inc(s_slots.sem, 1)
                link(tt(starts, ends, ntile, ALU.subtract))
                link(ts(starts, starts, float(P), None, ALU.mult))
                link(tt(slot, cum, starts.unsqueeze(1).broadcast_to([P, MT, E]), ALU.add))
                for w, o in ((0, o1), (1, o2)):
                    link(tt(prod.rearrange("p m g e -> p m (g e)"), slot, o.rearrange("p m g e -> p m (g e)"), ALU.mult))
                    link(nc.vector.tensor_reduce(slotf[:, w * MT:(w + 1) * MT], prod.rearrange("p m g e -> p m (g e)"),
                                                 AX_X, ALU.add))
                link(nc.vector.tensor_copy(slots[:].rearrange("p w m -> p (w m)"), slotf),
                     ts(slotd, slotf, 1.0 / P, None, ALU.mult))
                tiles = cst[:, C_IOTA:C_IOTA + NT * E:E].unsqueeze(1).broadcast_to([P, 2 * MT, NT])
                link(tt(slot_ge, slotd.unsqueeze(2).broadcast_to([P, 2 * MT, NT]), tiles, ALU.is_ge))
                link(nc.vector.tensor_reduce(slotn, slot_ge, AX_X, ALU.add),
                     tt(slot_hi[:, :, 0:NT - 1], slot_ge[:, :, 0:NT - 1], slot_ge[:, :, 1:NT], ALU.subtract),
                     nc.vector.tensor_copy(slot_hi[:, :, NT - 1:NT], slot_ge[:, :, NT - 1:NT]))
                link(nc.vector.scalar_tensor_tensor(out=slotn, in0=slotn, scalar=-float(P), in1=slotf, op0=ALU.mult, op1=ALU.add))
                number = cst[:, C_TOK:C_TOK + MT].unsqueeze(2).broadcast_to([P, MT, NT])
                link(*[tt(slot_hi[:, w * MT:(w + 1) * MT, :], slot_hi[:, w * MT:(w + 1) * MT, :], number, ALU.mult)
                       for w in range(2)])
                tt(slot_lo, slotn.unsqueeze(2).broadcast_to([P, 2 * MT, P]),
                   cst[:, C_LO:C_LO + P].unsqueeze(1).broadcast_to([P, 2 * MT, P]), ALU.is_equal).then_inc(s_oneh.sem, 1)
                dve.wait_ge(s_idt.sem, s_idt.at(l, 1))
                nc.vector.tensor_copy(idall[:], ps[:, 3, 0:NT]).then_inc(s_ids.sem, 1)
                for w, o in ((0, o1), (1, o2)):
                    link(tt(prod, sc4, o, ALU.mult))
                    link(nc.vector.tensor_reduce(wsel[:, w, :], prod.rearrange("p m g e -> p m (g e)"), AX_X, ALU.add))
                link(tt(wsel[:, 2, :], wsel[:, 0, :], wsel[:, 1, :], ALU.add))
                link(nc.vector.reciprocal(wsel[:, 3, :], wsel[:, 2, :]))
                for w in range(2):
                    link(tt(wsel[:, w, :], wsel[:, w, :], wsel[:, 3, :], ALU.mult))

            def experts(l):
                def gathered(i, b):
                    t = 2 * i + b
                    dve.wait_ge(s_mt[l], t + 1)
                    nc.vector.tensor_copy(xgT[l][b][:, 4:8, :], ps[:, 1, :].rearrange("p (c t) -> p c t", c=4))\
                        .then_inc(s_xed[l], 1)

                def silu(i, b):
                    t = 2 * i + b
                    dve.wait_ge(s_ex[l], t + 1)
                    ts(ebuf[b], ebuf[b], 1.0, None, ALU.add).then_inc(s_mc[l], 1)
                    dve.wait_ge(s_mc[l], 3 * t + 1)
                    nc.vector.reciprocal(ebuf[b], ebuf[b]).then_inc(s_mc[l], 1)
                    dve.wait_ge(s_mc[l], 3 * t + 2)
                    tt(ebuf[b], ps[:, 2 + b, 0:2 * P], ebuf[b], ALU.mult).then_inc(s_mc[l], 1)
                    dve.wait_ge(s_mc[l], 3 * t + 3)
                    tt(aT[b], ps[:, 2 + b, 2 * P:4 * P], ebuf[b], ALU.mult).then_inc(s_act[l], 1)

                def out_rows(i, b):
                    dve.wait_ge(s_dn[l], 2 * i + b + 1)
                    dve.wait_ge(s_yw[l][b], 16 * i + 16)
                    nc.vector.tensor_copy(yr[b][:, 512:D], ps[:, 5 + 2 * b, :]).then_inc(s_yed[l], 1)

                dve.sem_inc(s_yed[l], 2)
                gathered(0, 0)
                silu(0, 0)
                gathered(0, 1)
                with dve.Fori(0, NP - 1) as i:
                    silu(i, 1)
                    gathered(i + 1, 0)
                    out_rows(i, 0)
                    silu(i + 1, 0)
                    gathered(i + 1, 1)
                    out_rows(i, 1)
                silu(NP - 1, 1)
                gathered(NP, 0)
                out_rows(NP - 1, 0)
                silu(NP, 0)
                out_rows(NP - 1, 1)
                out_rows(NP, 0)

            def combine(l, m):
                a, b = yc[2 * m], yc[2 * m + 1]
                dve.wait_ge(s_ya.sem, s_ya.at(l, m + 1))
                link(nc.vector.scalar_tensor_tensor(out=a, in0=b, scalar=wsel[:, 1, m:m + 1], in1=a,
                                                    op0=ALU.mult, op1=ALU.add))
                link(tt(a, a, gate[cond(m)], ALU.mult))
                tt(x_rows[:, m, :], x_rows[:, m, :], a, ALU.add).then_inc(s_comb[l], 1)

            prow_a, prow_b = view(ST, 8 * KB, 512), view(ST, 10 * KB, 512)
            dve.wait_ge(s_about, 64)
            attention(0)
            out_and_norm2(0)
            route(0)
            ada(1)
            experts(0)

            dve.wait_ge(s_adast, 32)
            dve.wait_ge(ld_gate2.sem, ld_gate2.at(0, 32))
            for m in range(MT + 2):
                if m < MT:
                    combine(0, m)
                if m >= 2:
                    norm1_evac(1, m - 2)
                if 1 <= m <= MT:
                    dve.wait_ge(s_ss.sem, s_ss.at(1, m))
                    variance(m - 1, 1, D, out=s_var.sem)
                    normed(1, m - 1)


            def sw_transposed(m):
                dve.wait_ge(s_swt, 3 * m + 2)
                nc.vector.tensor_copy(qsT[:, 4:8, m * P:(m + 1) * P], ps[:, 1, :].rearrange("p (c t) -> p c t", c=4))\
                    .then_inc(s_swtd, 1)

            v = "p (h d) -> p h d"
            for m in range(MT):
                for o in range(3):
                    n = 3 * m + o
                    dve.wait_ge(s_swp, n + 1)
                    if n:
                        dve.wait_ge(s_swd, n)
                    if o == 0 and m:
                        sw_transposed(m - 1)
                        dve.wait_ge(s_swt, 3 * m)
                    src = ps[:, 4 + n % 4, :]
                    if o < 2:
                        row = qsrow[:, o * 512:(o + 1) * 512]
                        if m == PROMPT:
                            ins = nc.vector.tensor_copy(row, src)
                        else:
                            ins = rope(row.rearrange(v, d=64), src.rearrange(v, d=64), m, 64, 8)
                        ins.then_inc(s_swd, 1)
                        continue
                    kt = PROMPT_KT if m == PROMPT else m
                    ks = src[:, 0:256].rearrange(v, d=64)
                    if m == PROMPT:
                        link(nc.vector.tensor_copy(ksrow[:, :, 0, :], ks))
                    else:
                        link(rope(ksrow[:, :, 0, :], ks, m, 64, 4))
                    link(nc.vector.tensor_copy(vs[:, kt, :], src[:, 256:512]),
                         nc.vector.tensor_copy(ksrow[:, :, 1, :], ksrow[:, :, 0, :]))
                    dve.sem_inc(s_swd, 1)
                    dve.sem_inc(s_swrow, 1)
            sw_transposed(MT - 1)
            dve.wait_ge(s_swout, 32)
            attention(1)
            out_and_norm2(1)
            route(1)
            experts(1)

            dve.wait_ge(ld_gate2.sem, ld_gate2.at(1, 32))
            dve.wait_ge(ld_fg, 16)
            for m in range(MT + 1):
                if m < MT:
                    combine(1, m)
                if m:
                    u = m - 1
                    dve.wait_ge(s_fss, u + 1)
                    variance(u, 1, D, out=s_fvar)
                    dve.wait_ge(s_fr, u + 1)
                    nc.vector.scalar_tensor_tensor(out=x_rows[:, u, :], in0=x_rows[:, u, :], scalar=rstd[:, u:u + 1],
                                                   in1=bc[1][:, 0, :], op0=ALU.mult, op1=ALU.mult).then_inc(s_fy, 1)

        @block.tensor
        def _(pe):
            mm = nc.tensor.matmul
            pe.wait_ge(s_csil, 1)
            pe.wait_ge(ld_cst, 16)

            def ada(l, first, end):
                for n in range(first, end):
                    i = 12 * l + n
                    if n < 12:
                        pe.wait_ge(ld_ada[i % 3], 16 * (i // 3 + 1))
                        if i >= 2:
                            pe.wait_ge(s_adaev, i - 1)
                        for k in range(KC):
                            ins = mm(ps[0:2, 4 + i % 2, :], csil[:, :, k], ada_ring[l][i % 3][:, k, :],
                                     start=(k == 0), stop=(k == KC - 1))
                        ins.then_inc(s_adamm, 1)
                    if n:
                        pe.wait_ge(s_adaev, i)
                        for j in range(4):
                            at = 4 * (n - 1) + j
                            ins = nc.tensor.transpose(ps[:, l, at:at + 49:48],
                                                      ada_out[l][(i - 1) % 2][0:2, j * P:(j + 1) * P], ident[0:2, 0:2])
                        ins.then_inc(s_adatr, 1)

            def ada_finish(l):
                pe.wait_ge(s_adac, l + 1)
                nc.tensor.transpose(ps[0:96, 2 + l, 0:P], acol[l], ident).then_inc(s_adat, 1)
                pe.wait_ge(s_adar, l + 1)
                nc.tensor.transpose(ps[:, 4 + l, 0:96], arow[l][0:96, :], ident[0:96, 0:96]).then_inc(s_adat2, 1)
                pe.wait_ge(s_adacol, l + 1)

            def norm1(l):
                for m in range(MT):
                    pe.wait_ge(s_xn.sem, s_xn.at(l, m + 1))
                    if m >= 2:
                        pe.wait_ge(s_n1a.sem, s_n1a.at(l, m - 1))
                        pe.wait_ge(s_n1d.sem, s_n1d.at(l, m - 1))
                    for k in range(KC):
                        ins = nc.tensor.transpose(ps[:, (m % 2) * 2 + k // 4, (k % 4) * P:(k % 4 + 1) * P],
                                                  xn[l][m % 2][:, k * P:(k + 1) * P], ident)
                    ins.then_inc(s_n1t.sem, 1)
                pe.wait_ge(s_n1a.sem, s_n1a.at(l, MT))
                pe.wait_ge(s_n1d.sem, s_n1d.at(l, MT))

            ada(0, 0, 13)
            ada_finish(0)
            norm1(0)
            pe.wait_ge(ld_win, 64)

            def ab_bank_free(n):
                if n < 4:
                    return
                m, o = divmod(n - 4, 5)
                if o in (2, 3):
                    pe.wait_ge(s_abd, 2 * m + o - 1)
                else:
                    pe.wait_ge(s_aba, 3 * m + min(o, 2) + 1)

            def ab_transposes(m, q, k, ql, cv):
                if m:
                    pe.wait_ge(s_abta, 2 * m)
                    pe.wait_ge(s_abtd, 2 * m)
                for bank, row, n in ((0, q, 4), (1, k, 4), (2, ql, 3)):
                    if row is None:
                        continue
                    for c in range(n):
                        ins = nc.tensor.transpose(ps[:, bank, c * P:(c + 1) * P], row[:, c * P:(c + 1) * P], ident)
                    ins.then_inc(s_abt, 1)
                for c in range(2):
                    nc.tensor.transpose(ps[:, 3, c * P:(c + 1) * P], cv[:, c * P:(c + 1) * P], ident)
                nc.tensor.transpose(ps[0:KR, 3, 2 * P:3 * P], cv[:, CKV:CKV + KR], ident).then_inc(s_abt, 1)

            def ab_rows_ready(m):
                pe.wait_ge(s_abd, 2 * m + 2)
                pe.wait_ge(s_abrow, m + 1)

            for m in range(MT):
                for o, grp in enumerate(AB_ORDER):
                    n = 5 * m + o
                    at, w = AB_COLS[grp]
                    ab_bank_free(n)
                    for k in range(KC):
                        ins = mm(ps[:, 4 + n % 4, 0:w], hT[:, k, m * P:(m + 1) * P], w_in[:, k, at:at + w],
                                 start=(k == 0), stop=(k == KC - 1))
                    ins.then_inc(s_abp, 1)
                    if o == 1 and m:
                        ab_rows_ready(m - 1)
                        ab_transposes(m - 1, qrow, krow, qlrow, cvrow)
            ab_rows_ready(MT - 1)
            ab_transposes(MT - 1, qrow, krow, qlrow, cvrow)
            pe.wait_ge(ld_cache, 48)
            ab_transposes(MT, None, cache_k, None, cache_c)

            pe.wait_ge(ld_lat, 80)
            pe.wait_ge(s_aba, 3 * MT)
            pe.wait_ge(s_abta, 2 * MT + 1)
            pe.wait_ge(s_abtd, 2 * MT + 1)

            def qb_transposes(m):
                pe.wait_ge(s_qbr, m + 1)
                if m >= 2:
                    pe.wait_ge(s_qbta, m - 1)
                    pe.wait_ge(s_qbtd, m - 1)
                for h in range(MH):
                    ins = nc.tensor.transpose(ps[0:MQ, (m % 2) * 2 + h // 4, (h % 4) * P:(h % 4 + 1) * P],
                                              qbrow[m % 2][:, h * MQ:(h + 1) * MQ], ident)
                    if h % 4 == 3:
                        ins.then_inc(s_qbt, 1)

            for m in range(MT + 1):
                if m < MT:
                    for half in range(2):
                        j = 2 * m + half
                        if j >= 4:
                            pe.wait_ge(s_qba, j - 3)
                        for k in range(3):
                            ins = mm(ps[:, 4 + j % 4, 0:384], qlT[:, k, m * P:(m + 1) * P],
                                     wqb[:, k, half * 384:(half + 1) * 384], start=(k == 0), stop=(k == 2))
                        ins.then_inc(s_qbp, 1)
                if m:
                    qb_transposes(m - 1)
            pe.wait_ge(s_qba, 2 * MT)
            for n in range(14):
                is_v = n < 12 and n % 2 == 0
                if n >= 4:
                    b = n - 4
                    if b < 12 and b % 2 == 0:
                        pe.wait_ge(s_kva, b // 2 + 1)
                    else:
                        pe.wait_ge(s_kvd, b // 2 + 1)
                for k in range(2):
                    if is_v:
                        kt = n // 2
                        ins = mm(ps[:, 4 + n % 4, :], ckvT[:, k, kt * P:(kt + 1) * P], wkvb[:, k, 512:1024],
                                 start=(k == 0), stop=(k == 1))
                    else:
                        p, piece = divmod(n // 2 if n < 12 else n - 6, 2)
                        cols = slice(0, 512) if piece == 0 else slice(512, NKEY)
                        w = 512 if piece == 0 else NKEY - 512
                        ins = mm(ps[:, 4 + n % 4, 0:w], wkvb[:, k, p * P:(p + 1) * P], ckvT[:, k, cols],
                                 start=(k == 0), stop=(k == 1))
                ins.then_inc(s_kvp, 1)
            pe.wait_ge(s_kva, 6)
            pe.wait_ge(s_kvd, 8)
            pe.wait_ge(s_krc, 8)
            pe.wait_ge(s_qbta, MT)
            pe.wait_ge(s_qbtd, MT)
            pe.wait_ge(ld_vcache, 16)
            pe.wait_ge(s_about, 64)

            def attention(l):
                U = units[l]
                n = len(U)

                def times_values(u):
                    pe.wait_ge(s_ta.sem, s_ta.at(l, u + 1))
                    if wide(l, u + 1):
                        pe.wait_ge(s_td.sem, s_td.at(l, wide(l, u + 1)))
                    if u:
                        pe.wait_ge(s_oe.sem, s_oe.at(l, u))
                    pairs = (u + V_AFTER - X_AFTER + 1) // 2
                    if pairs > 0:
                        pe.wait_ge(s_xe.sem, s_xe.at(l, pairs))
                    kts = U[u][3]
                    for j, kt in enumerate(kts):
                        ins = mm(ps[:, 7, 0:v_width(U[u])], pT[u % 2][:, j, :], v_of(l, U[u], kt),
                                 start=(j == 0), stop=(j == len(kts) - 1))
                    ins.then_inc(s_o.sem, 1)

                for i in range(n + 5):
                    if i < n:
                        u = U[i]
                        if i >= 3:
                            pe.wait_ge(s_p.sem, s_p.at(l, i - 2))
                            if wide(l, i - 2):
                                pe.wait_ge(s_td.sem, s_td.at(l, wide(l, i - 2)))
                        for col, kt, w in pieces(u[3]):
                            ins = mm(score_row(i, SW)[:, col:col + w * P], q_of(l, u),
                                     k_of(l, u, kt, w), start=True, stop=True)
                        ins.then_inc(s_s.sem, 1)
                    for u in due(i, X_AFTER):
                        j = u // 2
                        pe.wait_ge(s_or.sem, s_or.at(l, j + 1))
                        pe.wait_ge(s_oe.sem, s_oe.at(l, min(i - V_AFTER, UNITS)))
                        if j:
                            pe.wait_ge(s_xe.sem, s_xe.at(l, j))
                        nc.tensor.transpose(ps[:, 7, P:2 * P], orow[:, j % 2, :], ident).then_inc(s_x.sem, 1)
                    for u in due(i, T_AFTER):
                        pe.wait_ge(s_p.sem, s_p.at(l, u + 1))
                        if u:
                            pe.wait_ge(s_ta.sem, s_ta.at(l, u))
                        for j in range(len(U[u][3])):
                            ins = nc.tensor.transpose(probs_t(u, j), prow[u % 3][:, j * P:(j + 1) * P], ident)
                        ins.then_inc(s_t.sem, 1)
                    for u in due(i, V_AFTER):
                        times_values(u)

            def out_and_router(l, w_out):
                pe.wait_ge(s_xe.sem, s_xe.at(l, len(units[l]) // 2))
                pe.wait_ge(ld_wout.sem, ld_wout.at(l, 16))
                for m in range(MT + 3):
                    if m < MT:
                        for half in range(2):
                            j = 2 * m + half
                            if j >= 4:
                                pe.wait_ge(s_oped.sem, s_oped.at(l, j - 3))
                            for k in range(KC):
                                ins = mm(ps[:, j % 4, :], hT[:, k, m * P:(m + 1) * P],
                                         w_out[:, k, half * 512:(half + 1) * 512], start=(k == 0), stop=(k == KC - 1))
                            ins.then_inc(s_op.sem, 1)
                    if 2 <= m <= MT + 1:
                        u = m - 2
                        pe.wait_ge(s_h2.sem, s_h2.at(l, u + 1))
                        if u:
                            pe.wait_ge(s_n2a.sem, s_n2a.at(l, u))
                            pe.wait_ge(s_n2d.sem, s_n2d.at(l, u))
                        for k in range(KC):
                            ins = nc.tensor.transpose(ps[:, 4 + k // 4, (k % 4) * P:(k % 4 + 1) * P],
                                                      xg[l][u % 2][:, k * P:(k + 1) * P], ident)
                        ins.then_inc(s_n2t.sem, 1)
                    if m >= 3:
                        u = m - 3
                        pe.wait_ge(s_n2a.sem, s_n2a.at(l, u + 1))
                        pe.wait_ge(s_n2d.sem, s_n2d.at(l, u + 1))
                        if u:
                            pe.wait_ge(s_rx.sem, s_rx.at(l, u))
                        for k in range(KC):
                            ins = mm(ps[:, 6, 0:E], xgT[l][u % 2][:, k, :], rw[:, k, :], start=(k == 0), stop=(k == KC - 1))
                        ins.then_inc(s_rt.sem, 1)
                pe.wait_ge(s_mask.sem, s_mask.at(l, 1))
                m80 = mask.rearrange("p m g e -> p (m g e)")
                mm(ps[:, 7, 0:80], tri, m80, start=True, stop=True)
                mm(ps[:, 7, 80:160], ones, m80, start=True, stop=True).then_inc(s_cnt.sem, 1)
                if l == 0:
                    ada(1, 0, 3)
                pe.wait_ge(s_oneh.sem, s_oneh.at(l, 1))
                for j in range(2 * MT):
                    ins = mm(ps[:, 3, 0:NT], slot_lo[:, j, :], slot_hi[:, j, :], start=(j == 0), stop=(j == 2 * MT - 1))
                ins.then_inc(s_idt.sem, 1)
                if l == 0:
                    ada(1, 3, 13)
                pe.wait_ge(s_ids.sem, s_ids.at(l, 1))
                if l == 0:
                    ada_finish(1)

            def experts(l):
                def gathered(i, b):
                    t = 2 * i + b
                    pe.wait_ge(s_xg[l][b], 16 * i + 16)
                    if not (isinstance(t, int) and t == 0):
                        pe.wait_ge(s_xea[l], t)
                        pe.wait_ge(s_xed[l], t)
                    for k in range(KC):
                        ins = nc.tensor.transpose(ps[:, k // 4, (k % 4) * P:(k % 4 + 1) * P],
                                                  xg[l][b][:, k * P:(k + 1) * P], ident)
                    ins.then_inc(s_mt[l], 1)

                def gate_up(i, b):
                    t = 2 * i + b
                    pe.wait_ge(s_wgu[l][b], 32 * i + 32)
                    pe.wait_ge(s_xea[l], t + 1)
                    pe.wait_ge(s_xed[l], t + 1)
                    for q, w in enumerate((wg[b], wg[b], wu[b], wu[b])):
                        for k in range(KC):
                            ins = mm(ps[:, 2 + b, q * P:(q + 1) * P], w[:, k, (q % 2) * P:(q % 2 + 1) * P],
                                     xgT[l][b][:, k, :], start=(k == 0), stop=(k == KC - 1))
                    ins.then_inc(s_gu[l], 1)

                def down(i, b):
                    t = 2 * i + b
                    pe.wait_ge(s_wd[l][b], 16 * i + 16)
                    pe.wait_ge(s_act[l], t + 1)
                    pe.wait_ge(s_yea[l], t + 1)
                    pe.wait_ge(s_yed[l], t + 1)
                    for half in range(2):
                        for q in range(2):
                            ins = mm(ps[:, 4 + 2 * b + half, :], aT[b][:, q * P:(q + 1) * P],
                                     wd[b][:, q, half * 512:(half + 1) * 512], start=(q == 0), stop=(q == 1))
                    ins.then_inc(s_dn[l], 1)

                gathered(0, 0)
                gate_up(0, 0)
                gathered(0, 1)
                with pe.Fori(0, NP - 1) as i:
                    gate_up(i, 1)
                    gathered(i + 1, 0)
                    down(i, 0)
                    gate_up(i + 1, 0)
                    gathered(i + 1, 1)
                    down(i, 1)
                gate_up(NP - 1, 1)
                gathered(NP, 0)
                down(NP - 1, 0)
                gate_up(NP, 0)
                down(NP - 1, 1)
                down(NP, 0)

            attention(0)
            out_and_router(0, w_abo)
            experts(0)
            norm1(1)

            def sw_transposes(m, q, k):
                if m:
                    pe.wait_ge(s_swta, 2 * m)
                    pe.wait_ge(s_swtd, m)
                if q is not None:
                    for c in range(KC):
                        ins = nc.tensor.transpose(ps[:, c // 4, (c % 4) * P:(c % 4 + 1) * P], q[:, c * P:(c + 1) * P], ident)
                        if c % 4 == 3:
                            ins.then_inc(s_swt, 1)
                for c in range(4):
                    ins = nc.tensor.transpose(ps[:, 2, c * P:(c + 1) * P], k[:, c * P:(c + 1) * P], ident)
                ins.then_inc(s_swt, 1)

            krows = ksrow.rearrange("p h t d -> p (h t d)")
            pe.wait_ge(ld_wswa, 16)
            for m in range(MT):
                for o in range(3):
                    n = 3 * m + o
                    if n >= 4:
                        pe.wait_ge(s_swd, n - 3)
                    for k in range(KC):
                        ins = mm(ps[:, 4 + n % 4, :], hT[:, k, m * P:(m + 1) * P], w_swa[:, k, o * 512:(o + 1) * 512],
                                 start=(k == 0), stop=(k == KC - 1))
                    ins.then_inc(s_swp, 1)
                    if o == 0 and m:
                        pe.wait_ge(s_swd, 3 * m)
                        sw_transposes(m - 1, qsrow, krows)
            pe.wait_ge(s_swd, 3 * MT)
            sw_transposes(MT - 1, qsrow, krows)
            pe.wait_ge(ld_scache, 48)
            sw_transposes(MT, None, cache_k)
            pe.wait_ge(s_swta, 2 * MT + 1)
            pe.wait_ge(s_swtd, MT)
            attention(1)
            out_and_router(1, w_swao)
            experts(1)


_INS = ['x_prompt', 'x_sample', 'cache_diff_k', 'cache_diff_v', 'cache_mla_ckv', 'cache_mla_krope', 'cache_swa_k',
        'cache_swa_v', 'c', 'c_ctx', 'ada_w', 'ada_b', 'norm1_g', 'norm2_g', 'final_norm_g', 'ab_w_in', 'diff_lambda',
        'diff_subln_g', 'mla_q_norm_g', 'mla_w_qb', 'mla_kv_norm_g', 'mla_w_kvb', 'ab_w_out', 'swa_w_in', 'swa_sink',
        'swa_w_out', 'router_w', 'router_bias', 'moe_w_gate', 'moe_w_up', 'moe_w_down']
_OUTS = [((1, 128, 1024), 'float32'), ((1, 512, 1024), 'float32'), ((1, 1, 128, 4, 2, 64), 'float32'),
         ((1, 1, 128, 4, 128), 'float32'), ((1, 1, 128, 256), 'float32'), ((1, 1, 128, 32), 'float32'),
         ((1, 1, 128, 4, 64), 'float32'), ((1, 1, 128, 4, 64), 'float32')]


def kernel(**inputs):
    import numpy as _np
    import concourse.bacc as _bacc
    from concourse import mybir as _mybir
    from concourse.bass_utils import run_bass_kernel_spmd as _run

    nc = _bacc.Bacc("TRN2", target_bir_lowering=False, num_devices=1)
    arrays, args = {}, []
    for name in _INS + ['consts']:
        a = constants() if name == 'consts' else _np.ascontiguousarray(inputs[name])
        arrays[f"in_{name}_dram"] = a
        args.append(nc.dram_tensor(f"in_{name}_dram", a.shape, _mybir.dt.from_np(a.dtype), kind="ExternalInput").ap())
    for i, (shape, dtype) in enumerate(_OUTS):
        dt = _mybir.dt.from_np(_np.dtype(dtype))
        args.append(nc.dram_tensor(f"out_{i}_dram", shape, dt, kind="ExternalOutput").ap())
    build(nc, *args)
    r = _run(nc, [arrays], core_ids=[0])
    return tuple(r.results[0][f"out_{i}_dram"] for i in range(len(_OUTS)))
```
